# Optimizing a Trainium2 kernel written in Bass

```python
import jax, jax.numpy as jnp
from jax import lax
import numpy as np

D_MODEL = 2048
BATCH = 1
SEQ = 256
DEPTH = 2

N_MIXERS = 2
EPS = 1e-6
CHUNK = 128
GMLP_WIDTH = D_MODEL
GMLP_GROUP = 128
GMLP_GROUPS = GMLP_WIDTH // GMLP_GROUP
HEAD_DIM = 128
HEADS_PER_GROUP = D_MODEL // 256
DILATION_CONFIGS = ((128, 1), (512, 4), (2048, 16))
N_DIL = len(DILATION_CONFIGS)
ATTN_WIDTH = HEADS_PER_GROUP * HEAD_DIM
QKV_WIDTH = 3 * N_DIL * ATTN_WIDTH
ROT_DIM = HEAD_DIM // 4
ROPE_THETA = 500000.0
FFN_DIM = 5632
CONV_WIDTH = 3

kernel_name = "hybrid_gmlp_dilated_attn_convffn"

def rms_norm(x, g):
    xf = x.astype(jnp.float32)
    y = xf * lax.rsqrt(jnp.mean(xf * xf, axis=-1, keepdims=True) + EPS)
    return (y * g.astype(jnp.float32)).astype(x.dtype)

def layer_norm(x, g, b):
    xf = x.astype(jnp.float32)
    mu = jnp.mean(xf, axis=-1, keepdims=True)
    xc = xf - mu
    var = jnp.mean(xc * xc, axis=-1, keepdims=True)
    y = xc * lax.rsqrt(var + EPS) * g.astype(jnp.float32) + b.astype(jnp.float32)
    return y.astype(x.dtype)

def rotary_tables(seq):
    pos = jnp.arange(seq, dtype=jnp.float32)
    inv = jnp.float32(ROPE_THETA) ** (-jnp.arange(0, ROT_DIM, 2, dtype=jnp.float32) / ROT_DIM)
    ang = pos[:, None] * inv[None, :]
    return jnp.cos(ang), jnp.sin(ang)

def apply_partial_rope(t, cos, sin):
    half = ROT_DIM // 2
    c = cos[None, :, None, None, :].astype(t.dtype)
    s = sin[None, :, None, None, :].astype(t.dtype)
    t1 = t[..., :half]
    t2 = t[..., half:ROT_DIM]
    return jnp.concatenate([t1 * c - t2 * s, t1 * s + t2 * c, t[..., ROT_DIM:]], axis=-1)

def gmlp_chunk_mixer(h, w_in, ln_g, ln_b, w_s, b_s, w_out):
    B, S, _ = h.shape
    z = jax.nn.gelu(h @ w_in)
    u, v = jnp.split(z, 2, axis=-1)
    v = layer_norm(v, ln_g, ln_b)
    vc = v.reshape(B, S // CHUNK, CHUNK, GMLP_GROUPS, GMLP_GROUP)
    causal = jnp.tril(jnp.ones((CHUNK, CHUNK), dtype=bool))
    ws = jnp.where(causal[None], w_s, 0).astype(v.dtype)
    mixed = jnp.einsum('gts,bnsgc->bntgc', ws, vc) + b_s.T[None, None, :, :, None].astype(v.dtype)
    return (u * mixed.reshape(B, S, GMLP_WIDTH)) @ w_out

def dilated_group_attention(q, k, v, window, dilation):
    B, S, H, E = q.shape
    d = dilation
    wb = window // dilation
    L = S // d
    nb = -(-L // wb)
    Lp = nb * wb
    pad_end = ((0, 0), (0, Lp - L), (0, 0), (0, 0), (0, 0))
    pad_front = ((0, 0), (wb, 0), (0, 0), (0, 0), (0, 0))

    def strided(t):
        return jnp.pad(t.reshape(B, L, d, H, E), pad_end)

    def context(t):
        tp = jnp.pad(t, pad_front).reshape(B, nb + 1, wb, d, H, E)
        return jnp.concatenate([tp[:, :-1], tp[:, 1:]], axis=2)

    qb = strided(q).reshape(B, nb, wb, d, H, E)
    kc = context(strided(k))
    vc = context(strided(v))
    s = jnp.einsum('bnqrhe,bnkrhe->bnrhqk', qb, kc).astype(jnp.float32) * (HEAD_DIM ** -0.5)
    qi = jnp.arange(wb)[:, None]
    kj = jnp.arange(2 * wb)[None, :]
    dist = wb + qi - kj
    band = (dist >= 0) & (dist <= wb)
    key_sub = jnp.arange(nb)[:, None] * wb - wb + jnp.arange(2 * wb)[None, :]
    mask = band[None] & (key_sub >= 0)[:, None, :]
    s = jnp.where(mask[None, :, None, None], s, -jnp.inf)
    m = jnp.max(s, axis=-1, keepdims=True)
    p = jnp.exp(s - m)
    den = jnp.sum(p, axis=-1, keepdims=True)
    lse = (m + jnp.log(den))[..., 0]
    o = jnp.einsum('bnrhqk,bnkrhe->bnqrhe', p / den, vc.astype(jnp.float32))
    o = o.reshape(B, Lp, d, H, E)[:, :L].reshape(B, S, H, E)
    lse = jnp.transpose(lse, (0, 1, 4, 2, 3)).reshape(B, Lp, d, H)[:, :L].reshape(B, S, H)
    return o, lse

def dilated_attention_mixer(h, w_qkv, w_o, cos, sin):
    B, S, _ = h.shape
    qkv = (h @ w_qkv).reshape(B, S, 3, N_DIL, HEADS_PER_GROUP, HEAD_DIM)
    q = apply_partial_rope(qkv[:, :, 0], cos, sin)
    k = apply_partial_rope(qkv[:, :, 1], cos, sin)
    v = qkv[:, :, 2]
    outs, lses = [], []
    for g, (window, dilation) in enumerate(DILATION_CONFIGS):
        o_g, l_g = dilated_group_attention(q[:, :, g], k[:, :, g], v[:, :, g], window, dilation)
        outs.append(o_g)
        lses.append(l_g)
    wts = jax.nn.softmax(jnp.stack(lses), axis=0)
    o = jnp.einsum('gbsh,gbshe->bshe', wts, jnp.stack(outs))
    return o.reshape(B, S, ATTN_WIDTH).astype(h.dtype) @ w_o

def conv_ffn(h, w_gate, w_up, conv_w, conv_b, w_down):
    g = h @ w_gate
    g = lax.conv_general_dilated(
        g, conv_w[:, None, :].astype(g.dtype), window_strides=(1,),
        padding=[(CONV_WIDTH - 1, 0)], dimension_numbers=('NWC', 'WIO', 'NWC'),
        feature_group_count=FFN_DIM) + conv_b.astype(g.dtype)
    return (jax.nn.silu(g) * (h @ w_up)) @ w_down

def setup_inputs(seed: int = 0) -> dict:
    key = jax.random.key(seed)
    ks = jax.random.split(key, 24)
    n_a = (DEPTH + 1) // 2
    n_b = DEPTH // 2
    f32 = jnp.float32

    def dense(k, shape, fan_in):
        return jax.random.normal(k, shape, f32) * (fan_in ** -0.5)

    def gain(k, shape):
        return 1.0 + 0.02 * jax.random.normal(k, shape, f32)

    return {
        "x": jax.random.normal(ks[0], (BATCH, SEQ, D_MODEL), f32),
        "a_ln": gain(ks[1], (n_a, D_MODEL)),
        "a_w_in": dense(ks[2], (n_a, D_MODEL, 2 * GMLP_WIDTH), D_MODEL),
        "a_sgu_ln_g": gain(ks[3], (n_a, GMLP_WIDTH)),
        "a_sgu_ln_b": 0.02 * jax.random.normal(ks[4], (n_a, GMLP_WIDTH), f32),
        "a_w_s": dense(ks[5], (n_a, GMLP_GROUPS, CHUNK, CHUNK), CHUNK),
        "a_b_s": gain(ks[6], (n_a, GMLP_GROUPS, CHUNK)),
        "a_w_out": dense(ks[7], (n_a, GMLP_WIDTH, D_MODEL), GMLP_WIDTH),
        "b_ln": gain(ks[8], (n_b, D_MODEL)),
        "b_w_qkv": dense(ks[9], (n_b, D_MODEL, QKV_WIDTH), D_MODEL),
        "b_w_o": dense(ks[10], (n_b, ATTN_WIDTH, D_MODEL), ATTN_WIDTH),
        "ffn_ln": gain(ks[11], (DEPTH, D_MODEL)),
        "ffn_w_gate": dense(ks[12], (DEPTH, D_MODEL, FFN_DIM), D_MODEL),
        "ffn_w_up": dense(ks[13], (DEPTH, D_MODEL, FFN_DIM), D_MODEL),
        "ffn_conv_w": dense(ks[14], (DEPTH, CONV_WIDTH, FFN_DIM), CONV_WIDTH),
        "ffn_conv_b": 0.02 * jax.random.normal(ks[15], (DEPTH, FFN_DIM), f32),
        "ffn_w_down": dense(ks[16], (DEPTH, FFN_DIM, D_MODEL), FFN_DIM),
        "final_ln": gain(ks[17], (D_MODEL,)),
    }

def reference(x, a_ln, a_w_in, a_sgu_ln_g, a_sgu_ln_b, a_w_s, a_b_s, a_w_out,
              b_ln, b_w_qkv, b_w_o, ffn_ln, ffn_w_gate, ffn_w_up, ffn_conv_w,
              ffn_conv_b, ffn_w_down, final_ln):
    cos, sin = rotary_tables(x.shape[1])
    h = x
    for i in range(DEPTH):
        j = i // N_MIXERS
        if i % N_MIXERS == 0:
            h = h + gmlp_chunk_mixer(rms_norm(h, a_ln[j]), a_w_in[j], a_sgu_ln_g[j],
                                     a_sgu_ln_b[j], a_w_s[j], a_b_s[j], a_w_out[j])
        else:
            h = h + dilated_attention_mixer(rms_norm(h, b_ln[j]), b_w_qkv[j], b_w_o[j], cos, sin)
        h = h + conv_ffn(rms_norm(h, ffn_ln[i]), ffn_w_gate[i], ffn_w_up[i],
                         ffn_conv_w[i], ffn_conv_b[i], ffn_w_down[i])
    return rms_norm(h, final_ln)


_drawn_inputs = setup_inputs


def setup_inputs(seed=0):
    import zlib

    import numpy as np

    out = dict(_drawn_inputs(seed))
    spreads = {}
    factors = {'a_ln': 3.035,
     'a_sgu_ln_g': 7.091,
     'a_sgu_ln_b': 6.998,
     'a_b_s': 4.583,
     'b_ln': 8.0,
     'ffn_ln': 3.277,
     'ffn_conv_b': 4.669,
     'final_ln': 2.82}
    for name, (base, spread) in spreads.items():
        noise = np.random.default_rng([zlib.crc32(name.encode()), seed]).standard_normal(out[name].shape)
        drawn = base * np.exp(spread * noise) if base else spread * noise
        out[name] = __import__('jax').numpy.asarray(drawn.astype(out[name].dtype))
    for name, factor in factors.items():
        out[name] = (out[name] * factor).astype(out[name].dtype)
    return out
```

```python
from contextlib import ExitStack

import numpy as np

import concourse.bass as bass
from concourse import mybir

F32 = mybir.dt.float32
F32R = mybir.dt.float32r
ACT = mybir.ActivationFunctionType
ALU = mybir.AluOpType
AX_X = mybir.AxisListType.X

P = 128
S = 256
D = 2048
KT = D // P
FFN = 5632
FB = FFN // P
HEADS = 8
GROUPS = 3
E = 128
CHUNK = 128
EPS = 1e-6
ROT = E // 4
HALF = ROT // 2
THETA = 500000.0
DILATIONS = ((128, 1), (512, 4), (2048, 16))
MASKED = -1e30

UT = 8
RING = 4
AHEAD = 2
UC = UT * P

U_V = 0
U_U = U_V + KT * KT // UT
U_AO = U_U + KT * KT // UT
U_F0 = U_AO + KT * KT // UT
U_D0 = U_F0 + 2 * FB * KT // UT
U_QKV = U_D0 + KT * FB // UT
HEAD_UNITS = 3 * GROUPS * KT // UT
U_WO = U_QKV + HEADS * HEAD_UNITS
U_F1 = U_WO + KT * HEADS // UT
U_D1 = U_F1 + 2 * FB * KT // UT
UNITS = U_D1 + KT * FB // UT
P_V = 0
P_U = P_V + KT // 2
P_AO = P_U + KT // 2
P_F0 = P_AO + KT // 2
P_D0 = P_F0 + FB
P_WO = P_D0 + KT // 2
P_F1 = P_WO + KT // 2
P_D1 = P_F1 + FB

C_ALN, C_SG, C_SB, C_BLN = 0, KT, 2 * KT, 3 * KT
C_FLN = 4 * KT
C_FIN = 6 * KT
C_CONV = 7 * KT
VECS = C_CONV + 2 * 4 * FB

GAINS = {0: C_ALN, 1: C_FLN, 2: C_BLN, 3: C_FLN + KT}
NORM_PAIRS = KT // 2


def pair_of(j):
    return bass.ds(2 * j, 2)


def one(c):
    return bass.ds(c, 1)


def gx_step(j):
    return 18 + 2 * j if j < NORM_PAIRS - 1 else 34


def wait_pos(eng, semaphore, value):
    if not isinstance(value, int) or value > 0:
        eng.wait_ge(semaphore, value)


Q0 = GROUPS * P
SC = Q0 + GROUPS * S


def trunk(nc, w_stream, x_t, vecs_d, ws_t, bs_row, mask_d, rope_d, out_t):
    with ExitStack() as ctx:
        def sb(name, shape, dt=F32):
            return ctx.enter_context(nc.sbuf_tensor(name, shape, dt))

        def sem(name):
            return ctx.enter_context(nc.semaphore(name))

        raw = [sb(f"raw{i}", [P, UC]) for i in range(RING)]
        w_hi = [sb(f"w_hi{i}", [P, UC], F32R) for i in range(RING)]
        w_lo = [sb(f"w_lo{i}", [P, UC], F32R) for i in range(RING)]
        h = sb("h", [P, KT, S])
        x_at = nc.sbuf_base
        X = sb("X", [P, KT, 2 * S], F32R)
        vecs = sb("vecs", [P, VECS])
        rinv = sb("rinv", [P, S])
        std = sb("std", [P, S])
        ssum = sb("ssum", [P, 2 * S])
        sq = sb("sq", [P, 2, S])
        mean_w = sb("mean_w", [P, P])
        eps = sb("eps", [P, 1])
        hc = sb("hc", [P, 2, S])
        tsum = sb("tsum", [P, 2, S])
        gu = sb("gu", [P, 2, S + 2])
        conv = sb("conv", [P, S])
        act_g = sb("act_g", [P, S])
        hidden = sb("hidden", [P, S])

        ident = sb("ident", [P, P])

        arena_at = nc.sbuf_base
        arena_bytes = FB * 2 * S * 4
        sb("arena", [P, FB * 2 * S])

        def place(name, at, shape, dt=F32):
            assert at + int(np.prod(shape[1:])) * 4 <= arena_bytes
            return nc.alloc_sbuf_tensor_at(name, shape, dt, offset=arena_at + at)

        hid = place("hid", 0, [P, FB, 2 * S], F32R)
        BLK = S * 4
        V = place("V", 0, [P, KT, S])
        U = place("U", KT * BLK, [P, KT, S])
        GX = place("GX", 2 * KT * BLK, [P, KT, 2 * S], F32R)
        at = 4 * KT * BLK
        WS = place("WS", at, [P, KT, P])
        BS = place("BS", at + 8 * BLK, [P, KT, P])
        at += 16 * BLK
        vn = [place(f"vn{i}", at + i * BLK, [P, S]) for i in range(2)]
        vt = [place(f"vt{i}", at + (2 + i) * BLK, [P, 2, P]) for i in range(2)]
        vsum = place("vsum", at + 4 * BLK, [P, 2, S])
        ln_rinv = place("ln_rinv", at + 6 * BLK, [P, S])
        OX = place("OX", 0, [P, HEADS, 2 * S], F32R)
        at = HEADS * 2 * BLK
        QK = [place(f"QK{i}", at + i * 6 * BLK, [P, GROUPS, 2, S]) for i in range(2)]
        at += 12 * BLK
        VT = [place(f"VT{i}", at + i * 3 * BLK, [P, GROUPS, 2, P]) for i in range(2)]
        at += 6 * BLK
        vrow = place("vrow", at, [P, S])
        swap = place("swap", at + BLK, [P, 2, S])
        rope = place("rope", at + 3 * BLK, [P, 2, S])
        at += 5 * BLK
        sm = place("sm", at, [P, SC])
        pt = place("pt", at + SC * 4, [P, SC])
        mask = place("mask", at + 2 * SC * 4, [P, SC])
        at += 3 * SC * 4
        nmax = place("nmax", at, [P, 2])
        rsum = place("rsum", at + 32, [P, 2])
        rrec = place("rrec", at + 64, [P, 2])
        Y = nc.alloc_sbuf_tensor_at("Y", [P, KT, S], F32, offset=x_at)

        acc = [ctx.enter_context(nc.psum_tensor(f"acc{i}", [P, 2, 2 * S], F32)) for i in range(2)]
        sc_ps = ctx.enter_context(nc.psum_tensor("sc_ps", [P, 3, 512], F32))
        sc_flat = sc_ps[:, :, :].rearrange("p b c -> p (b c)")
        misc = ctx.enter_context(nc.psum_tensor("misc", [P, 512], F32))
        turn_ps = [sc_ps[:, 0, 0:S], sc_ps[:, 1, 0:S]]
        mix_ps = [sc_ps[:, 2, 0:S], misc[:, 0:S]]
        Q1 = 512
        score_parts = ((0, Q0, 0), (Q0, SC, Q1))

        raw_landed = [sem(f"raw_landed{i}") for i in range(RING)]
        vecs_landed = sem("vecs_landed")
        x_landed = [sem(f"x_landed{i}") for i in range(4)]
        ws_landed = sem("ws_landed")
        bs_landed = sem("bs_landed")
        mask_landed = sem("mask_landed")
        rope_landed = sem("rope_landed")
        out_written = sem("out_written")
        hi_ready = sem("hi_ready")
        lo_ready = sem("lo_ready")
        units_done = sem("units_done")
        cleared = sem("cleared")
        ident_set = sem("ident_set")
        ws_masked = sem("ws_masked")
        hcopied = sem("hcopied")
        pair_summed = sem("pair_summed")
        pair_taken = sem("pair_taken")
        x_hi = sem("x_hi")
        x_ready = sem("x_ready")
        squared = sem("squared")
        ss_clear = sem("ss_clear")
        ss_added = sem("ss_added")
        ms_ready = sem("ms_ready")
        rms_ready = sem("rms_ready")
        rinv_ready = sem("rinv_ready")
        gelued = sem("gelued")
        v_added = sem("v_added")
        mean_ready = sem("mean_ready")
        centered = sem("centered")
        vss_clear = sem("vss_clear")
        ln_squared = sem("ln_squared")
        ln_added = sem("ln_added")
        var_ready = sem("var_ready")
        ln_std = sem("ln_std")
        ln_rinv_ready = sem("ln_rinv_ready")
        vn_scaled = sem("vn_scaled")
        vn_ready = sem("vn_ready")
        vn_turned = sem("vn_turned")
        vt_ready = sem("vt_ready")
        mixed = sem("mixed")
        mix_ready = sem("mix_ready")
        gated = sem("gated")
        gx_hi = sem("gx_hi")
        gx_ready = sem("gx_ready")
        tap2 = sem("tap2")
        tap1 = sem("tap1")
        tap0 = sem("tap0")
        silued = sem("silued")
        hid_made = sem("hid_made")
        hid_hi = sem("hid_hi")
        hid_ready = sem("hid_ready")
        qk_hcopied = sem("qk_hcopied")
        qk_summed = sem("qk_summed")
        qk_taken = sem("qk_taken")
        swapped = sem("swapped")
        rope_sin = sem("rope_sin")
        rope_cos = sem("rope_cos")
        roped = sem("roped")
        swap_clear = sem("swap_clear")
        vh_hcopied = sem("vh_hcopied")
        vh_summed = sem("vh_summed")
        vh_taken = sem("vh_taken")
        vh_turned = sem("vh_turned")
        vh_ready = sem("vh_ready")
        scored = sem("scored")
        masked = sem("masked")
        maxed = sem("maxed")
        exped = sem("exped")
        rsum_inv = sem("rsum_inv")
        normed = sem("normed")
        p_turned = sem("p_turned")
        pt_ready = sem("pt_ready")
        attended = sem("attended")
        o_hi = sem("o_hi")
        o_ready = sem("o_ready")
        y_ready = sem("y_ready")
        y_done = sem("y_done")

        def vec(c):
            return vecs[:, c:c + 1]

        def over(ap, n):
            return ap[:, None, :].broadcast_to([P, n, S])

        block = ctx.enter_context(nc.Block())

        @block.sync
        def _(sp):
            def load(u, q, slot):
                sp.dma_start(raw[slot][:, :], w_stream[u, :, :]).then_inc(raw_landed[slot], 16)

            for slot in range(RING):
                load(slot, 0, slot)
            with sp.Fori(1, UNITS // RING) as q:
                for slot in range(RING):
                    sp.wait_ge(lo_ready, RING * q + (slot + 1 - RING))
                    load(RING * q + slot, q, slot)
            for c in range(4):
                sp.wait_ge(y_done, c + 1)
                sp.dma_start(out_t[:, 4 * c:4 * c + 4, :], Y[:, 4 * c:4 * c + 4, :]).then_inc(out_written, 16)
            sp.wait_ge(out_written, 4 * 16)

        @block.gpsimd
        def _(pool):
            nc.gpsimd.memset(mean_w[:, :], 1.0 / D).then_inc(cleared, 1)
            nc.gpsimd.memset(eps[:, :], EPS).then_inc(cleared, 1)
            nc.gpsimd.memset(gu[:, :, 0:2], 0.0).then_inc(cleared, 1)
            nc.gpsimd.memset(vsum[:, :, :], 0.0).then_inc(cleared, 1)
            nc.gpsimd.memset(ident[:, :], 0.0).then_inc(cleared, 1)
            pool.wait_ge(cleared, 5)
            nc.gpsimd.affine_select(out=ident[:, :], in_=ident[:, :], compare_op=ALU.not_equal, fill=1.0,
                                    base=0, pattern=[[-1, P]], channel_multiplier=1).then_inc(ident_set, 1)

            def norm_sums(n, pairs):
                if n:
                    pool.wait_ge(ms_ready, n)
                nc.gpsimd.memset(ssum[:, :], 0.0).then_inc(ss_clear, 1)
                pool.wait_ge(ss_clear, n + 1)
                with pool.Fori(0, pairs) as i:
                    pool.wait_ge(squared, pairs * n + 1 + i)
                    if n:
                        pool.wait_ge(ss_added, pairs * n + i)
                    nc.gpsimd.tensor_tensor(ssum[:, :], ssum[:, :], sq[:, :, :].rearrange("p a b -> p (a b)"),
                                            ALU.add).then_inc(ss_added, 1)

            def first_sums():
                nc.gpsimd.memset(ssum[:, :], 0.0).then_inc(ss_clear, 1)
                pool.wait_ge(ss_clear, 1)
                for i in range(KT // 2):
                    pool.wait_ge(squared, 1 + i)
                    if i:
                        pool.wait_ge(ss_added, i)
                    nc.gpsimd.tensor_tensor(ssum[:, :], ssum[:, :], sq[:, :, :].rearrange("p a b -> p (a b)"),
                                            ALU.add).then_inc(ss_added, 1)

            first_sums()
            pool.wait_ge(ws_landed, 16)
            nc.gpsimd.affine_select(out=WS[:, :, :], in_=WS[:, :, :], compare_op=ALU.is_ge, fill=0.0,
                                    base=0, pattern=[[0, KT], [1, P]], channel_multiplier=-1).then_inc(ws_masked, 1)
            for p in range(KT // 2):
                pool.wait_ge(gelued, p + 1)
                if p:
                    pool.wait_ge(v_added, p)
                nc.gpsimd.tensor_tensor(vsum[:, :, :], vsum[:, :, :], V[:, 2 * p:2 * p + 2, :], ALU.add)\
                    .then_inc(v_added, 1)
            pool.wait_ge(mean_ready, 1)
            nc.gpsimd.memset(vsum[:, :, :], 0.0).then_inc(vss_clear, 1)
            pool.wait_ge(vss_clear, 1)
            for c in range(4):
                pool.wait_ge(ln_squared, c + 1)
                for k in range(2):
                    if c or k:
                        pool.wait_ge(ln_added, 2 * c + k)
                    nc.gpsimd.tensor_tensor(vsum[:, :, :], vsum[:, :, :], U[:, 12 + 2 * k:14 + 2 * k, :], ALU.add)\
                        .then_inc(ln_added, 1)
            for j in range(KT // 2):
                pool.wait_ge(gelued, P_U + j + 1)
                pool.wait_ge(mix_ready, 2 * j + 2)
                nc.gpsimd.tensor_tensor(U[:, 2 * j:2 * j + 2, :], U[:, 2 * j:2 * j + 2, :],
                                        V[:, 2 * j:2 * j + 2, :], ALU.mult).then_inc(gated, 1)
            norm_sums(1, KT // 2)
            norm_sums(2, KT // 2)
            pool.wait_ge(units_done, U_QKV)
            pool.dma_start(rope[:, :, :], rope_d).then_inc(rope_landed, 16)
            pool.dma_start(mask[:, :], mask_d).then_inc(mask_landed, 16)
            nc.gpsimd.memset(swap[:, :, :], 0.0).then_inc(swap_clear, 1)
            norm_sums(3, KT // 2)
            norm_sums(4, KT // 2)

        @block.scalar
        def _(act):
            def split_step(first, s, rounds=0):
                c = first + s + AHEAD
                slot, q = c % RING, rounds + c // RING
                act.wait_ge(raw_landed[slot], 16 * q + 16)
                wait_pos(act, units_done, RING * rounds + (c + 1 - RING))
                nc.scalar.activation(w_hi[slot][:, :], raw[slot][:, :], ACT.Copy).then_inc(hi_ready, 1)

            def settled():
                act.wait_ge(vecs_landed, 16)

            def high_copy(pair, s, done):
                act.wait_ge(units_done, done)
                wait_pos(act, pair_summed, pair)
                nc.scalar.activation(hc[:, :, :], acc[s][:, :, 0:S], ACT.Copy).then_inc(hcopied, 1)

            def square_pair(n, pr):
                nc.scalar.activation(sq[:, :, :], h[:, pair_of(pr), :], ACT.Square).then_inc(squared, 1)

            def norm_pair(n, pr):
                wait_pos(act, ss_added, NORM_PAIRS * n + pr)
                settled()
                for b in range(2):
                    nc.scalar.activation(X[:, 2 * pr + b, 0:S], h[:, 2 * pr + b, :], ACT.Copy,
                                         scale=vecs[:, one(GAINS[n] + 2 * pr + b)]).then_inc(x_hi, 1)
                square_pair(n, pr)

            def rms(n):
                act.wait_ge(ms_ready, n + 1)
                nc.scalar.activation(std[:, :], misc[:, 0:S], ACT.Sqrt, bias=eps[:, :]).then_inc(rms_ready, 1)

            def gelu_evac(pair, pr, stage, s, dst, done):
                if stage == 0:
                    high_copy(pair, s, done)
                if stage == 1:
                    act.wait_ge(pair_taken, pair + 1)
                    settled()
                    nc.scalar.activation(dst[:, pair_of(pr), :], gu[:, :, 2:S + 2], ACT.Gelu_apprx_tanh)\
                        .then_inc(gelued, 1)

            def residual(n, pair, pr, stage, s, done):
                if stage == 0:
                    high_copy(pair, s, done)
                if stage == 1:
                    act.wait_ge(pair_taken, pair + 1)
                    if n < 4:
                        norm_pair(n, pr)
                    else:
                        act.wait_ge(ss_added, NORM_PAIRS * n + pr)
                        for b in range(2):
                            nc.scalar.activation(Y[:, 2 * pr + b, :], h[:, 2 * pr + b, :], ACT.Copy,
                                                 scale=vecs[:, one(C_FIN + 2 * pr + b)]).then_inc(y_ready, 1)
                        square_pair(n, pr)

            def ffn_evac(layer, pair, j, stage, s, done):
                f = FB * layer + j
                cv = C_CONV + 4 * FB * layer
                if stage == 0:
                    high_copy(pair, s, done)
                if stage == 1:
                    act.wait_ge(pair_taken, pair + 1)
                    wait_pos(act, silued, f)
                    settled()
                    nc.scalar.activation(conv[:, :], gu[:, 0, 2:S + 2], ACT.Identity,
                                         bias=vecs[:, one(cv + 3 * FB + j)],
                                         scale=vecs[:, one(cv + 2 * FB + j)]).then_inc(tap2, 1)
                if stage == 2:
                    act.wait_ge(tap0, f + 1)
                    wait_pos(act, hid_made, f)
                    nc.scalar.activation(act_g[:, :], conv[:, :], ACT.Silu).then_inc(silued, 1)
                if stage == 3:
                    act.wait_ge(hid_made, f + 1)
                    settled()
                    nc.scalar.activation(hid[:, j, 0:S], hidden[:, :], ACT.Copy).then_inc(hid_hi, 1)

            def ffn(layer, u0, p0, ud, pd):
                rms(1 + 2 * layer)
                with act.Fori(0, FB // 2) as i:
                    for s in range(4, 12):
                        c = s // 4 - 1
                        split_step(u0, s, rounds=2 * i)
                        ffn_evac(layer, p0 + 2 * i + c, 2 * i + c, s % 4, c, u0 + 8 * i + 4 * (c + 1))

                def down(i, s, split):
                    c = s // 11 - 1
                    if split:
                        split_step(ud, s, rounds=11 * i)
                    if c >= 0 and s % 11 < 2:
                        residual(2 + 2 * layer, pd + 4 * i + c, 4 * i + c, s % 11, c % 2, ud + 44 * i + 11 * (c + 1))

                if layer == 0:
                    with act.Fori(0, 2) as i:
                        for s in range(4, 48):
                            down(i, s, True)
                else:
                    for i in range(2):
                        for s in range(4, 48):
                            down(i, s, ud + 44 * i + s + AHEAD < UNITS)

            act.dma_start(vecs[:, :], vecs_d).then_inc(vecs_landed, 16)
            for c in range(4):
                act.dma_start(h[:, 4 * c:4 * c + 4, :], x_t[:, 4 * c:4 * c + 4, :]).then_inc(x_landed[c], 16)
            act.dma_start(WS[:, :, :], ws_t).then_inc(ws_landed, 16)
            act.dma_start(BS[:, :, :].rearrange("p a b -> p (a b)"), bs_row.partition_broadcast(P))\
               .then_inc(bs_landed, 16)
            act.wait_ge(vecs_landed, 16)
            act.wait_ge(cleared, 5)
            for pr in range(NORM_PAIRS):
                act.wait_ge(x_landed[pr // 2], 16)
                norm_pair(0, pr)
                if pr == 1:
                    split_step(U_V, -2)
                if pr == 5:
                    split_step(U_V, -1)
            for s in range(4):
                split_step(U_V, s)
            rms(0)
            with act.Fori(0, KT // 4) as i:
                for s in range(4, 12):
                    c = s // 4 - 1
                    split_step(U_V, s, rounds=2 * i)
                    gelu_evac(P_V + 2 * i + c, 2 * i + c, s % 4, c, V, U_V + 8 * i + 4 * (c + 1))
            for k in range(4, KT * KT // UT + 4):
                split_step(U_U, k)
                j = k // 4 - 1
                if j == 6 and k % 4 == 1:
                    act.wait_ge(ln_added, 8)
                gelu_evac(P_U + j, j, k % 4, j % 2, U, U_U + 4 * (j + 1))
                if 5 <= k < 9:
                    c = k - 5
                    act.wait_ge(centered, c + 1)
                    wait_pos(act, ln_added, 2 * c)
                    nc.scalar.activation(U[:, 12:16, :], V[:, 4 * c:4 * c + 4, :], ACT.Square).then_inc(ln_squared, 1)
                if k == 10:
                    act.wait_ge(var_ready, 1)
                    nc.scalar.activation(std[:, :], misc[:, S:2 * S], ACT.Sqrt, bias=eps[:, :]).then_inc(ln_std, 1)
                g = k - 14
                if 0 <= g < KT:
                    act.wait_ge(vn_turned, g + 1)
                    wait_pos(act, mixed, g - 1)
                    nc.scalar.activation(vt[g % 2][:, :, :].rearrange("p a b -> p (a b)"),
                                         turn_ps[g % 2], ACT.Copy).then_inc(vt_ready, 1)
                for jg in range(NORM_PAIRS):
                    if k == gx_step(jg):
                        act.wait_ge(gated, jg + 1)
                        nc.scalar.activation(GX[:, pair_of(jg), 0:S], U[:, pair_of(jg), :], ACT.Copy).then_inc(gx_hi, 1)
            with act.Fori(0, KT // 4) as i:
                for s in range(4, 12):
                    c = s // 4 - 1
                    split_step(U_AO, s, rounds=2 * i)
                    residual(1, P_AO + 2 * i + c, 2 * i + c, s % 4, c, U_AO + 8 * i + 4 * (c + 1))
            ffn(0, U_F0, P_F0, U_D0, P_D0)

            def qk_evac(h_, g, stage, par):
                gi = GROUPS * h_ + g
                if stage == 0:
                    act.wait_ge(units_done, U_QKV + HEAD_UNITS * h_ + 6 * g + 4)
                    wait_pos(act, vh_summed, gi)
                    nc.scalar.activation(hc[:, :, :], acc[0][:, :, 0:S], ACT.Copy).then_inc(qk_hcopied, 1)
                if stage == 1:
                    act.wait_ge(qk_taken, gi + 1)
                    act.wait_ge(swap_clear, 1)
                    wait_pos(act, roped, gi)
                    nc.scalar.activation(swap[0:HALF, :, :], QK[par][2 * HALF:3 * HALF, g, :, :], ACT.Copy)\
                        .then_inc(swapped, 1)
                    nc.scalar.activation(swap[2 * HALF:3 * HALF, :, :], QK[par][0:HALF, g, :, :], ACT.Copy)\
                        .then_inc(swapped, 1)

            def v_evac(h_, g):
                gi = GROUPS * h_ + g
                act.wait_ge(units_done, U_QKV + HEAD_UNITS * h_ + 6 * g + 6)
                act.wait_ge(qk_summed, gi + 1)
                nc.scalar.activation(hc[:, 0, :], acc[1][:, 0, 0:S], ACT.Copy).then_inc(vh_hcopied, 1)

            def v_turn(h_, g, par):
                gi = GROUPS * h_ + g
                act.wait_ge(vh_turned, gi + 1)
                if g == 0:
                    wait_pos(act, attended, h_ - 1)
                nc.scalar.activation(VT[par][:, g, :, :].rearrange("p a b -> p (a b)"), misc[:, S:2 * S], ACT.Copy)\
                    .then_inc(vh_ready, 1)

            def softmax_exp(h_):
                for t, (a, b, _) in enumerate(score_parts):
                    act.wait_ge(maxed, 2 * h_ + t + 1)
                    nc.scalar.activation(sm[:, a:b], sm[:, a:b], ACT.Exp, bias=nmax[:, t:t + 1],
                                         accum_out=rsum[:, t:t + 1]).then_inc(exped, 1)

            def p_turn(h_):
                act.wait_ge(p_turned, h_ + 1)
                wait_pos(act, attended, h_)
                for a, b, c in score_parts:
                    nc.scalar.activation(pt[:, a:b], sc_flat[:, c:c + b - a], ACT.Copy).then_inc(pt_ready, 1)

            def head_out(h_):
                act.wait_ge(attended, h_ + 1)
                settled()
                nc.scalar.activation(OX[:, h_, 0:S], acc[1][:, 1, 0:S], ACT.Copy).then_inc(o_hi, 1)

            def head_step(h_, par, t, before, rounds=0, c0=0):
                split_step(U_QKV + c0, t, rounds=rounds)
                if before and t == 0:
                    v_evac(h_ - 1, 2)
                if before and t == 2:
                    v_turn(h_ - 1, 2, 1 - par)
                if before and t == 3:
                    softmax_exp(h_ - 1)
                if t % 6 == 0 and t:
                    v_evac(h_, t // 6 - 1)
                if t % 6 == 2 and t > 2:
                    v_turn(h_, t // 6 - 1, par)
                if t % 6 >= 4:
                    qk_evac(h_, t // 6, t % 6 - 4, par)
                if before and t == 9:
                    p_turn(h_ - 1)
                if before and t == 13:
                    head_out(h_ - 1)

            rms(2)
            for t in range(4, HEAD_UNITS):
                head_step(0, 0, t, False)
            with act.Fori(0, 3) as i:
                for k in range(2):
                    for t in range(HEAD_UNITS):
                        head_step(2 * i + 1 + k, 1 - k, t, True, rounds=9 * i, c0=HEAD_UNITS * (1 + k))
            last = HEADS - 1
            for t in range(HEAD_UNITS):
                head_step(last, 1, t, True, c0=HEAD_UNITS * last)
            for s in range(2):
                split_step(U_WO, s)
            v_evac(last, 2)
            v_turn(last, 2, 1)
            softmax_exp(last)
            p_turn(last)
            head_out(last)
            with act.Fori(0, 4) as i:
                for s in range(2, 6):
                    c = s // 2 - 1
                    split_step(U_WO, s, rounds=i)
                    residual(3, P_WO + 2 * i + c, 2 * i + c, s % 2, c, U_WO + 4 * i + 2 * (c + 1))
            for s in range(2, 4):
                split_step(U_F1, s)
            ffn(1, U_F1, P_F1, U_D1, P_D1)
            rms(4)

        @block.vector
        def _(dve):
            def split_step(first, s, rounds=0):
                c = first + s + AHEAD
                slot = c % RING
                dve.wait_ge(hi_ready, RING * rounds + c + 1)
                nc.vector.tensor_tensor(w_lo[slot][:, :], raw[slot][:, :], w_hi[slot][:, :], ALU.subtract)\
                    .then_inc(lo_ready, 1)

            def sum_pair(pair, s):
                dve.wait_ge(hcopied, pair + 1)
                wait_pos(dve, pair_taken, pair)
                nc.vector.tensor_tensor(tsum[:, :, :], hc[:, :, :], acc[s][:, :, S:2 * S], ALU.add)\
                    .then_inc(pair_summed, 1)

            def inverse_rms(n):
                dve.wait_ge(rms_ready, n + 1)
                nc.vector.reciprocal(rinv[:, :], std[:, :]).then_inc(rinv_ready, 1)
                dve.wait_ge(rinv_ready, n + 1)

            def x_low(n, pr):
                for b in range(2):
                    dve.wait_ge(x_hi, KT * n + 2 * pr + b + 1)
                    nc.vector.scalar_tensor_tensor(X[:, 2 * pr + b, S:2 * S], h[:, 2 * pr + b, :],
                                                   vecs[:, one(GAINS[n] + 2 * pr + b)], X[:, 2 * pr + b, 0:S],
                                                   ALU.mult, ALU.subtract).then_inc(x_ready, 1)

            def scale_pair(pair, s, in_use, uses):
                sum_pair(pair, s)
                dve.wait_ge(pair_summed, pair + 1)
                wait_pos(dve, in_use, uses)
                nc.vector.tensor_tensor(gu[:, :, 2:S + 2], tsum[:, :, :], over(rinv, 2), ALU.mult)\
                    .then_inc(pair_taken, 1)

            def residual(n, pair, pr, stage, s):
                if stage == 0:
                    sum_pair(pair, s)
                    dve.wait_ge(pair_summed, pair + 1)
                    nc.vector.tensor_tensor(h[:, pair_of(pr), :], h[:, pair_of(pr), :], tsum[:, :, :], ALU.add)\
                        .then_inc(pair_taken, 1)
                if stage == 1 and n < 4:
                    x_low(n, pr)

            def ffn_evac(layer, pair, j, stage, s):
                f = FB * layer + j
                cv = C_CONV + 4 * FB * layer
                if stage == 0:
                    scale_pair(pair, s, hid_made, f)
                if stage == 1:
                    dve.wait_ge(tap2, f + 1)
                    nc.vector.scalar_tensor_tensor(conv[:, :], gu[:, 0, 1:S + 1], vecs[:, one(cv + FB + j)], conv[:, :],
                                                   ALU.mult, ALU.add).then_inc(tap1, 1)
                    dve.wait_ge(tap1, f + 1)
                    nc.vector.scalar_tensor_tensor(conv[:, :], gu[:, 0, 0:S], vecs[:, one(cv + j)], conv[:, :],
                                                   ALU.mult, ALU.add).then_inc(tap0, 1)
                if stage == 2:
                    dve.wait_ge(silued, f + 1)
                    wait_pos(dve, hid_ready, f)
                    nc.vector.tensor_tensor(hidden[:, :], act_g[:, :], gu[:, 1, 2:S + 2], ALU.mult)\
                        .then_inc(hid_made, 1)
                if stage == 3:
                    dve.wait_ge(hid_hi, f + 1)
                    nc.vector.tensor_tensor(hid[:, j, S:2 * S], hidden[:, :], hid[:, j, 0:S], ALU.subtract)\
                        .then_inc(hid_ready, 1)

            def ffn(layer, u0, p0, ud, pd):
                inverse_rms(1 + 2 * layer)
                with dve.Fori(0, FB // 2) as i:
                    for s in range(4, 12):
                        c = s // 4 - 1
                        split_step(u0, s, rounds=2 * i)
                        ffn_evac(layer, p0 + 2 * i + c, 2 * i + c, s % 4, c)

                def down(i, s, split):
                    c = s // 11 - 1
                    if split:
                        split_step(ud, s, rounds=11 * i)
                    if c >= 0 and s % 11 < 2:
                        residual(2 + 2 * layer, pd + 4 * i + c, 4 * i + c, s % 11, c % 2)

                if layer == 0:
                    with dve.Fori(0, 2) as i:
                        for s in range(4, 48):
                            down(i, s, True)
                else:
                    for i in range(2):
                        for s in range(4, 48):
                            down(i, s, ud + 44 * i + s + AHEAD < UNITS)

            dve.wait_ge(vecs_landed, 16)
            for pr in range(NORM_PAIRS):
                x_low(0, pr)
                if pr == 1:
                    split_step(U_V, -2)
                if pr == 5:
                    split_step(U_V, -1)
            for s in range(4):
                split_step(U_V, s)
            inverse_rms(0)
            with dve.Fori(0, KT // 4) as i:
                for s in range(4, 12):
                    c = s // 4 - 1
                    split_step(U_V, s, rounds=2 * i)
                    if s % 4 == 0:
                        scale_pair(P_V + 2 * i + c, c, gelued, P_V + 2 * i + c)
            for k in range(4, KT * KT // UT + 4):
                split_step(U_U, k)
                j = k // 4 - 1
                if k % 4 == 0:
                    scale_pair(P_U + j, j % 2, gelued, P_U + j)
                if 4 <= k < 8:
                    c = k - 4
                    dve.wait_ge(mean_ready, 1)
                    nc.vector.tensor_tensor(V[:, 4 * c:4 * c + 4, :], V[:, 4 * c:4 * c + 4, :],
                                            over(misc[:, 0:S], 4), ALU.subtract).then_inc(centered, 1)
                if k == 11:
                    dve.wait_ge(ln_std, 1)
                    nc.vector.reciprocal(ln_rinv[:, :], std[:, :]).then_inc(ln_rinv_ready, 1)
                    dve.wait_ge(ln_rinv_ready, 1)
                g = k - 12
                if 0 <= g < KT:
                    wait_pos(dve, vn_turned, g - 1)
                    nc.vector.scalar_tensor_tensor(vn[g % 2][:, :], V[:, g, :], vec(C_SG + g), ln_rinv[:, :],
                                                   ALU.mult, ALU.mult).then_inc(vn_scaled, 1)
                    dve.wait_ge(vn_scaled, g + 1)
                    nc.vector.tensor_scalar(vn[g % 2][:, :], vn[g % 2][:, :], vec(C_SB + g), None, ALU.add)\
                        .then_inc(vn_ready, 1)
                g = k - 16
                if 0 <= g < KT:
                    dve.wait_ge(mixed, g + 1)
                    if g == 0:
                        dve.wait_ge(bs_landed, 16)
                    nc.vector.tensor_tensor(V[:, g, :].rearrange("p (n t) -> p n t", n=2),
                                            mix_ps[g % 2].rearrange("p (n t) -> p n t", n=2),
                                            BS[:, g, None, :].broadcast_to([P, 2, P]), ALU.add).then_inc(mix_ready, 1)
                for jg in range(NORM_PAIRS):
                    if k == gx_step(jg):
                        dve.wait_ge(gx_hi, jg + 1)
                        nc.vector.tensor_tensor(GX[:, pair_of(jg), S:2 * S], U[:, pair_of(jg), :],
                                                GX[:, pair_of(jg), 0:S], ALU.subtract).then_inc(gx_ready, 1)
            with dve.Fori(0, KT // 4) as i:
                for s in range(4, 12):
                    c = s // 4 - 1
                    split_step(U_AO, s, rounds=2 * i)
                    residual(1, P_AO + 2 * i + c, 2 * i + c, s % 4, c)
            ffn(0, U_F0, P_F0, U_D0, P_D0)

            def qk_evac(h_, g, stage, par):
                gi = GROUPS * h_ + g
                if stage == 0:
                    dve.wait_ge(qk_hcopied, gi + 1)
                    wait_pos(dve, vh_taken, gi)
                    nc.vector.tensor_tensor(tsum[:, :, :], hc[:, :, :], acc[0][:, :, S:2 * S], ALU.add)\
                        .then_inc(qk_summed, 1)
                    dve.wait_ge(qk_summed, gi + 1)
                    if g == 0:
                        wait_pos(dve, scored, h_ - 1)
                    nc.vector.tensor_tensor(QK[par][:, g, :, :], tsum[:, :, :], over(rinv, 2), ALU.mult)\
                        .then_inc(qk_taken, 1)
                if stage == 1:
                    rows = 3 * HALF
                    dve.wait_ge(rope_landed, 16)
                    dve.wait_ge(swapped, 2 * gi + 2)
                    nc.vector.tensor_tensor(swap[0:rows, :, :], swap[0:rows, :, :],
                                            rope[0:rows, 1, None, :].broadcast_to([rows, 2, S]), ALU.mult)\
                        .then_inc(rope_sin, 1)
                    nc.vector.tensor_tensor(QK[par][0:rows, g, :, :], QK[par][0:rows, g, :, :],
                                            rope[0:rows, 0, None, :].broadcast_to([rows, 2, S]), ALU.mult)\
                        .then_inc(rope_cos, 1)
                    dve.wait_ge(rope_sin, gi + 1)
                    dve.wait_ge(rope_cos, gi + 1)
                    nc.vector.tensor_tensor(QK[par][0:rows, g, :, :], QK[par][0:rows, g, :, :], swap[0:rows, :, :],
                                            ALU.add).then_inc(roped, 1)

            def v_evac(h_, g):
                gi = GROUPS * h_ + g
                dve.wait_ge(vh_hcopied, gi + 1)
                dve.wait_ge(qk_taken, gi + 1)
                nc.vector.tensor_tensor(tsum[:, 0, :], hc[:, 0, :], acc[1][:, 0, S:2 * S], ALU.add)\
                    .then_inc(vh_summed, 1)
                dve.wait_ge(vh_summed, gi + 1)
                wait_pos(dve, vh_turned, gi)
                nc.vector.tensor_tensor(vrow[:, :], tsum[:, 0, :], rinv[:, :], ALU.mult).then_inc(vh_taken, 1)

            def mask_scores(h_):
                dve.wait_ge(mask_landed, 16)
                dve.wait_ge(scored, h_ + 1)
                wait_pos(dve, p_turned, h_)
                for a, b, c in score_parts:
                    nc.vector.scalar_tensor_tensor(sm[:, a:b], sc_flat[:, c:c + b - a], float(E) ** -0.5, mask[:, a:b],
                                                   ALU.mult, ALU.add).then_inc(masked, 1)
                for t, (a, b, _) in enumerate(score_parts):
                    dve.wait_ge(masked, 2 * h_ + t + 1)
                    nc.vector.reduce_max(nmax[:, t:t + 1], sm[:, a:b], AX_X, negate=True).then_inc(maxed, 1)

            def normalize(h_):
                dve.wait_ge(exped, 2 * h_ + 2)
                nc.vector.reciprocal(rrec[:, :], rsum[:, :]).then_inc(rsum_inv, 1)
                dve.wait_ge(rsum_inv, h_ + 1)
                for t, (a, b, _) in enumerate(score_parts):
                    nc.vector.tensor_scalar(sm[:, a:b], sm[:, a:b], rrec[:, t:t + 1], None, ALU.mult)\
                        .then_inc(normed, 1)

            def head_out(h_):
                dve.wait_ge(o_hi, h_ + 1)
                nc.vector.tensor_tensor(OX[:, h_, S:2 * S], acc[1][:, 1, 0:S], OX[:, h_, 0:S], ALU.subtract)\
                    .then_inc(o_ready, 1)

            def head_step(h_, par, t, before, rounds=0, c0=0):
                split_step(U_QKV + c0, t, rounds=rounds)
                if before and t == 0:
                    v_evac(h_ - 1, 2)
                if before and t == 3:
                    mask_scores(h_ - 1)
                if t % 6 == 0 and t:
                    v_evac(h_, t // 6 - 1)
                if before and t == 6:
                    normalize(h_ - 1)
                if t % 6 >= 4:
                    qk_evac(h_, t // 6, t % 6 - 4, par)
                if before and t == 13:
                    head_out(h_ - 1)

            inverse_rms(2)
            for t in range(4, HEAD_UNITS):
                head_step(0, 0, t, False)
            with dve.Fori(0, 3) as i:
                for k in range(2):
                    for t in range(HEAD_UNITS):
                        head_step(2 * i + 1 + k, 1 - k, t, True, rounds=9 * i, c0=HEAD_UNITS * (1 + k))
            last = HEADS - 1
            for t in range(HEAD_UNITS):
                head_step(last, 1, t, True, c0=HEAD_UNITS * last)
            for s in range(2):
                split_step(U_WO, s)
            v_evac(last, 2)
            mask_scores(last)
            normalize(last)
            head_out(last)
            with dve.Fori(0, 4) as i:
                for s in range(2, 6):
                    c = s // 2 - 1
                    split_step(U_WO, s, rounds=i)
                    residual(3, P_WO + 2 * i + c, 2 * i + c, s % 2, c)
            for s in range(2, 4):
                split_step(U_F1, s)
            ffn(1, U_F1, P_F1, U_D1, P_D1)
            inverse_rms(4)
            dve.wait_ge(y_ready, KT)
            for c in range(4):
                nc.vector.tensor_tensor(Y[:, 4 * c:4 * c + 4, :], Y[:, 4 * c:4 * c + 4, :], over(rinv, 4), ALU.mult)\
                    .then_inc(y_done, 1)

        @block.tensor
        def _(pe):
            def multiply(u, slot, tiles, needs=None):
                pe.wait_ge(lo_ready, u + 1)
                for n, (bank, moving, kt, first, last) in enumerate(tiles):
                    if needs:
                        needs(kt)
                    hi = w_hi[slot][:, n * P:(n + 1) * P]
                    lo = w_lo[slot][:, n * P:(n + 1) * P]
                    if not last:
                        nc.tensor.matmul(bank, hi, moving[:, kt, :], start=first, stop=False)
                        op = nc.tensor.matmul(bank[:, S:2 * S], lo, moving[:, kt, 0:S], start=False, stop=False)
                    else:
                        nc.tensor.matmul(bank[:, S:2 * S], lo, moving[:, kt, 0:S], start=False, stop=False)
                        op = nc.tensor.matmul(bank, hi, moving[:, kt, :], start=False, stop=True)
                op.then_inc(units_done, 1)

            def tiles_of(pair_set, moving, k_tiles, n):
                at = [n * UT + t for t in range(UT)]
                return [(acc[pair_set][:, a // k_tiles, :], moving, a % k_tiles, a % k_tiles == 0,
                         a % k_tiles == k_tiles - 1) for a in at]

            def two_pairs(u, pair, moving, k_tiles, needs=None, after=None):
                per = 2 * k_tiles // UT
                for n in range(2 * per):
                    if n % per == 0:
                        wait_pos(pe, pair_summed, pair + n // per - 1)
                    multiply(u + n, n % RING, tiles_of(n // per, moving, k_tiles, n % per),
                             needs if n < k_tiles // UT else None)
                    if after:
                        after(n)

            def mean_square(n):
                pe.wait_ge(ss_added, NORM_PAIRS * (n + 1))
                for b in range(2):
                    op = nc.tensor.matmul(misc[:, 0:S], mean_w[:, :], ssum[:, b * S:(b + 1) * S],
                                          start=(b == 0), stop=(b == 1))
                op.then_inc(ms_ready, 1)

            def normed_ready(n):
                return lambda kt: pe.wait_ge(x_ready, KT * n + kt + 1)

            def product(u0, p0, pairs, moving, k_tiles, needs, n=None):
                two_pairs(u0, p0, moving, k_tiles, needs, (lambda k: mean_square(n) if k == 2 else None)
                          if n is not None else None)
                per = 4 * k_tiles // UT
                with pe.Fori(1, pairs // 2) as i:
                    two_pairs(u0 + per * i, p0 + 2 * i, moving, k_tiles)

            def down(layer, ud, pd):
                with pe.Fori(0, 2) as i:
                    pe.wait_ge(hid_ready, FB * (layer + 1) - 1)
                    for c in range(4):
                        wait_pos(pe, pair_summed, pd + 4 * i + c - 1)
                        for n in range(11):
                            def needs(kt, c=c, n=n):
                                if c == 0 and n < 6 and kt == FB - 1:
                                    pe.wait_ge(hid_ready, FB * (layer + 1))
                            multiply(ud + 44 * i + 11 * c + n, (11 * c + n) % RING, tiles_of(c % 2, hid, FB, n), needs)

            pe.wait_ge(cleared, 5)
            pe.wait_ge(ident_set, 1)
            product(U_V, P_V, KT // 2, X, KT, normed_ready(0), 0)

            for k in range(KT * KT // UT):
                if k % 4 == 0:
                    pe.wait_ge(pair_summed, P_U + k // 4 - 1)
                multiply(U_U + k, k % RING, tiles_of(k // 4 % 2, X, KT, k % 4))
                if k == 2:
                    pe.wait_ge(v_added, KT // 2)
                    for b in range(2):
                        op = nc.tensor.matmul(misc[:, 0:S], mean_w[:, :], vsum[:, b, :], start=(b == 0), stop=(b == 1))
                    op.then_inc(mean_ready, 1)
                if k == 9:
                    pe.wait_ge(ln_added, 8)
                    for b in range(2):
                        op = nc.tensor.matmul(misc[:, S:2 * S], mean_w[:, :], vsum[:, b, :], start=(b == 0), stop=(b == 1))
                    op.then_inc(var_ready, 1)
                g = k - 15
                if 0 <= g < KT:
                    pe.wait_ge(vt_ready, g + 1)
                    wait_pos(pe, mix_ready, g - 1)
                    pe.wait_ge(ws_masked, 1)
                    for n in range(2):
                        op = nc.tensor.matmul(mix_ps[g % 2][:, P * n:P * (n + 1)],
                                              vt[g % 2][:, n, :], WS[:, g, :], start=True, stop=True)
                    op.then_inc(mixed, 1)
                g = k - 13
                if 0 <= g < KT:
                    pe.wait_ge(vn_ready, g + 1)
                    wait_pos(pe, vt_ready, g - 1)
                    for n in range(2):
                        op = nc.tensor.transpose(turn_ps[g % 2][:, P * n:P * (n + 1)],
                                                 vn[g % 2][:, P * n:P * (n + 1)], ident[:, :])
                    op.then_inc(vn_turned, 1)

            def gx_needed(kt):
                if kt % 2 == 0:
                    pe.wait_ge(gx_ready, kt // 2 + 1)

            product(U_AO, P_AO, KT // 2, GX, KT, gx_needed)
            product(U_F0, P_F0, FB, X, KT, normed_ready(1), 1)
            down(0, U_D0, P_D0)

            def v_turn(h_, g):
                gi = GROUPS * h_ + g
                pe.wait_ge(vh_taken, gi + 1)
                wait_pos(pe, vh_ready, gi)
                for n in range(2):
                    op = nc.tensor.transpose(misc[:, S + P * n:S + P * (n + 1)], vrow[:, P * n:P * (n + 1)], ident[:, :])
                op.then_inc(vh_turned, 1)

            def scores(h_, par):
                pe.wait_ge(roped, GROUPS * (h_ + 1))
                wait_pos(pe, pt_ready, 2 * h_)
                for g in range(GROUPS):
                    q, k = QK[par][:, g, 0, :], QK[par][:, g, 1, :]
                    nc.tensor.matmul(sc_flat[:, P * g:P * (g + 1)], q[:, 0:P], k[:, 0:P], start=True, stop=True)
                    op = nc.tensor.matmul(sc_flat[:, Q1 + S * g:Q1 + S * (g + 1)], q[:, P:S], k, start=True, stop=True)
                op.then_inc(scored, 1)

            def p_turn(h_):
                pe.wait_ge(normed, 2 * h_ + 2)
                for a, b, c in score_parts:
                    for n in range((b - a) // P):
                        op = nc.tensor.transpose(sc_flat[:, c + P * n:c + P * (n + 1)], sm[:, a + P * n:a + P * (n + 1)],
                                                 ident[:, :])
                op.then_inc(p_turned, 1)

            def attend(h_, par):
                pe.wait_ge(pt_ready, 2 * h_ + 2)
                pe.wait_ge(vh_ready, GROUPS * (h_ + 1))
                wait_pos(pe, o_ready, h_)
                for g in range(GROUPS):
                    nc.tensor.matmul(acc[1][:, 1, 0:P], VT[par][:, g, 0, :], pt[:, P * g:P * (g + 1)],
                                     start=(g == 0), stop=(g == GROUPS - 1))
                for g in range(GROUPS):
                    for n in range(2):
                        c = Q0 + S * g + P * n
                        op = nc.tensor.matmul(acc[1][:, 1, P:S], VT[par][:, g, n, :], pt[:, c:c + P],
                                              start=(g == 0 and n == 0), stop=(g == GROUPS - 1 and n == 1))
                op.then_inc(attended, 1)

            def head(h_, par, before, u, needs=None, first=False):
                for t in range(HEAD_UNITS):
                    g, b = t // 6, t % 6 // 2
                    gi = GROUPS * h_ + g
                    if t % 6 == 0:
                        wait_pos(pe, qk_summed, gi)
                    if t % 6 == 4:
                        wait_pos(pe, vh_summed, gi)
                    bank = acc[0][:, b, :] if b < 2 else acc[1][:, 0, :]
                    kts = [(t % 2) * UT + n for n in range(UT)]
                    slot = (t + (0 if par == 0 else HEAD_UNITS)) % RING
                    multiply(u + t, slot, [(bank, X, kt, kt == 0, kt == KT - 1) for kt in kts],
                             needs if t < 2 else None)
                    if first and t == 2:
                        mean_square(2)
                    if before and t == 1:
                        v_turn(h_ - 1, 2)
                    if before and t == 2:
                        scores(h_ - 1, 1 - par)
                    if t % 6 == 1 and t > 1:
                        v_turn(h_, g - 1)
                    if before and t == 8:
                        p_turn(h_ - 1)
                    if before and t == 12:
                        attend(h_ - 1, 1 - par)

            pe.wait_ge(pair_summed, P_WO)
            head(0, 0, False, U_QKV, normed_ready(2), first=True)
            with pe.Fori(0, 3) as i:
                for k in range(2):
                    head(2 * i + 1 + k, 1 - k, True, U_QKV + HEAD_UNITS * (1 + k) + 2 * HEAD_UNITS * i)
            last = HEADS - 1
            head(last, 1, True, U_QKV + HEAD_UNITS * last)
            v_turn(last, 2)
            scores(last, 1)
            p_turn(last)
            attend(last, 1)
            pe.wait_ge(vh_summed, GROUPS * HEADS)
            pe.wait_ge(o_ready, HEADS)
            product(U_WO, P_WO, KT // 2, OX, HEADS, None)
            product(U_F1, P_F1, FB, X, KT, normed_ready(3), 3)
            down(1, U_D1, P_D1)
            mean_square(4)


def blocks(w):
    k, n = w.shape
    return w.reshape(k // P, P, n // P, P).transpose(2, 0, 1, 3)


def head_order():
    first, second, rest = list(range(HALF)), list(range(HALF, ROT)), list(range(ROT, E))
    return first + rest[:HALF] + second + rest[HALF:]


def stream(a_w_in, a_w_out, b_w_qkv, b_w_o, gate, up, down):
    w_in = blocks(a_w_in)
    ffn = [np.stack([blocks(g), blocks(u)], 1) for g, u in zip(gate, up)]
    qkv = b_w_qkv.reshape(D, 3, GROUPS, HEADS, E).transpose(3, 2, 1, 0, 4)
    qk = qkv[:, :, 0:2][..., np.array(head_order())]
    qkv = np.concatenate([qk, qkv[:, :, 2:]], 2)
    parts = [w_in[KT:], w_in[:KT], blocks(a_w_out), ffn[0], blocks(down[0]),
             qkv.reshape(-1, P, E), blocks(b_w_o), ffn[1], blocks(down[1])]
    tiles = np.concatenate([p.reshape(-1, P, P) for p in parts])
    return np.ascontiguousarray(tiles.reshape(UNITS, UT, P, P).transpose(0, 2, 1, 3)).reshape(UNITS, P, UC)


def columns(v):
    return v.reshape(-1, P).T


def rope_table():
    inv = np.float32(THETA) ** (-np.arange(0, ROT, 2, dtype=np.float32) / np.float32(ROT))
    ang = (np.arange(S, dtype=np.float32)[:, None] * inv[None, :].astype(np.float32)).T
    table = np.zeros((P, 2, S), np.float32)
    table[:, 0] = 1.0
    table[0:HALF, 0] = table[2 * HALF:3 * HALF, 0] = np.cos(ang)
    table[0:HALF, 1] = -np.sin(ang)
    table[2 * HALF:3 * HALF, 1] = np.sin(ang)
    return table


def mask_table():
    out = []
    for qt in range(2):
        for window, dilation in DILATIONS:
            dist = (P * qt + np.arange(P))[:, None] - np.arange(P * (qt + 1))[None, :]
            seen = (dist >= 0) & (dist <= window) & (dist % dilation == 0)
            out.append(np.where(seen, np.float32(0), np.float32(MASKED)))
    return np.concatenate(out, 1).astype(np.float32)


def kernel(x, a_ln, a_w_in, a_sgu_ln_g, a_sgu_ln_b, a_w_s, a_b_s, a_w_out, b_ln, b_w_qkv, b_w_o,
           ffn_ln, ffn_w_gate, ffn_w_up, ffn_conv_w, ffn_conv_b, ffn_w_down, final_ln):
    import concourse.bacc as bacc
    from concourse.bass_utils import run_bass_kernel_spmd

    f = np.asarray
    conv = [columns(v) for layer in range(2) for v in (*f(ffn_conv_w)[layer], f(ffn_conv_b)[layer])]
    arrays = {
        "w_stream": stream(f(a_w_in)[0], f(a_w_out)[0], f(b_w_qkv)[0], f(b_w_o)[0],
                           f(ffn_w_gate), f(ffn_w_up), f(ffn_w_down)),
        "x_t": f(x)[0].T.reshape(KT, P, S).transpose(1, 0, 2),
        "vecs_d": np.concatenate([columns(f(v)) for v in (a_ln[0], a_sgu_ln_g[0], a_sgu_ln_b[0], b_ln[0], ffn_ln[0],
                                                          ffn_ln[1], final_ln)] + conv, 1),
        "ws_t": f(a_w_s)[0].transpose(2, 0, 1),
        "bs_row": f(a_b_s)[0].reshape(1, -1),
        "mask_d": mask_table(),
        "rope_d": rope_table(),
    }
    nc = bacc.Bacc("TRN2", target_bir_lowering=False, num_devices=1)
    arrays = {name: np.ascontiguousarray(a) for name, a in arrays.items()}
    args = [nc.dram_tensor(name, a.shape, F32, kind="ExternalInput").ap() for name, a in arrays.items()]
    out_t = nc.dram_tensor("out_t", (P, KT, S), F32, kind="ExternalOutput").ap()
    trunk(nc, *args, out_t)
    r = run_bass_kernel_spmd(nc, [arrays], core_ids=[0])
    got = np.asarray(r.results[0]["out_t"])
    return got.transpose(1, 0, 2).reshape(D, S).T.reshape(1, S, D)
```

```python
from contextlib import ExitStack

import numpy as np

import concourse.bass as bass
from concourse import mybir

F32 = mybir.dt.float32
F32R = mybir.dt.float32r
ACT = mybir.ActivationFunctionType
ALU = mybir.AluOpType
AX_X = mybir.AxisListType.X

P = 128
S = 256
D = 2048
KT = D // P
FFN = 5632
FB = FFN // P
HEADS = 8
GROUPS = 3
E = 128
CHUNK = 128
EPS = 1e-6
ROT = E // 4
HALF = ROT // 2
THETA = 500000.0
DILATIONS = ((128, 1), (512, 4), (2048, 16))
MASKED = -1e30

UT = 8
RING = 4
AHEAD = 2
UC = UT * P

U_V = 0
U_U = U_V + KT * KT // UT
U_AO = U_U + KT * KT // UT
U_F0 = U_AO + KT * KT // UT
U_D0 = U_F0 + 2 * FB * KT // UT
U_QKV = U_D0 + KT * FB // UT
HEAD_UNITS = 3 * GROUPS * KT // UT
U_WO = U_QKV + HEADS * HEAD_UNITS
U_F1 = U_WO + KT * HEADS // UT
U_D1 = U_F1 + 2 * FB * KT // UT
UNITS = U_D1 + KT * FB // UT
P_V = 0
P_U = P_V + KT // 2
P_AO = P_U + KT // 2
P_F0 = P_AO + KT // 2
P_D0 = P_F0 + FB
P_QKV = P_D0 + KT // 2
HEAD_PAIRS = 5
P_WO = P_QKV + HEADS * HEAD_PAIRS
P_F1 = P_WO + KT // 2
P_D1 = P_F1 + FB

X_LOADS = (2, 2, 4, 4, 4)
X_PAIRS = [load for load, n in enumerate(X_LOADS) for _ in range(n // 2)]
POOL_PAIRS = 4

C_ALN, C_SG, C_SB, C_BLN = 0, KT, 2 * KT, 3 * KT
C_FLN = 4 * KT
C_FIN = 6 * KT
C_CONV = 7 * KT
VECS = C_CONV + 2 * 4 * FB

ADDED_F0 = KT // 2
ADDED_QKV = 2 * (KT // 2)
ADDED_F1 = 3 * (KT // 2)

GAINS = {0: C_ALN, 1: C_FLN, 2: C_BLN, 3: C_FLN + KT}
NORM_PAIRS = KT // 2


def pair_of(j):
    return bass.ds(2 * j, 2)


def one(c):
    return bass.ds(c, 1)


def gx_step(j):
    return 19 + 2 * j if j < NORM_PAIRS - 1 else 33


def wait_pos(eng, semaphore, value):
    if not isinstance(value, int) or value > 0:
        eng.wait_ge(semaphore, value)


Q0 = GROUPS * P
SC = Q0 + GROUPS * S


def trunk(nc, w_stream, x_t, vecs_d, ws_t, bs_row, mask_d, rope_d, out):
    with ExitStack() as ctx:
        def sb(name, shape, dt=F32):
            return ctx.enter_context(nc.sbuf_tensor(name, shape, dt))

        def sem(name):
            return ctx.enter_context(nc.semaphore(name))

        raw = [sb(f"raw{i}", [P, UC]) for i in range(RING)]
        w_hi = [sb(f"w_hi{i}", [P, UC], F32R) for i in range(RING)]
        w_lo = [sb(f"w_lo{i}", [P, UC], F32R) for i in range(RING)]
        h = sb("h", [P, KT, S])
        x_at = nc.sbuf_base
        X = sb("X", [P, KT, 2 * S], F32R)
        vecs = sb("vecs", [P, VECS])
        rinv = sb("rinv", [P, S])
        std = sb("std", [P, S])
        ssum = sb("ssum", [P, 2 * S])
        sq = sb("sq", [P, 2, S])
        mean_w = sb("mean_w", [P, P])
        eps = sb("eps", [P, 1])
        hc = sb("hc", [P, 2, S])
        tsum = sb("tsum", [P, 2, S])
        gu = sb("gu", [P, 2, S + 2])
        conv = sb("conv", [P, S])
        act_g = sb("act_g", [P, S])
        hidden = sb("hidden", [P, S])

        ident = sb("ident", [P, P])
        fin_std = sb("fin_std", [P, 2])
        fin_rinv = sb("fin_rinv", [P, 2])

        arena_at = -(-nc.sbuf_base // 32) * 32
        arena_bytes = FB * 2 * S * 4
        sb("arena", [P, FB * 2 * S])

        def place(name, at, shape, dt=F32):
            assert at + int(np.prod(shape[1:])) * 4 <= arena_bytes
            return nc.alloc_sbuf_tensor_at(name, shape, dt, offset=arena_at + at)

        hid = place("hid", 0, [P, FB, 2 * S], F32R)
        BLK = S * 4
        V = place("V", 0, [P, KT, S])
        U = place("U", KT * BLK, [P, KT, S])
        GX = place("GX", 2 * KT * BLK, [P, KT, 2 * S], F32R)
        at = 4 * KT * BLK
        WS = place("WS", at, [P, KT, P])
        BS = place("BS", at + 8 * BLK, [P, KT, P])
        at += 16 * BLK
        vn = [place(f"vn{i}", at + i * BLK, [P, S]) for i in range(2)]
        vt = [place(f"vt{i}", at + (2 + i) * BLK, [P, 2, P]) for i in range(2)]
        vsum = place("vsum", at + 4 * BLK, [P, 2, S])
        ln_rinv = place("ln_rinv", at + 6 * BLK, [P, S])
        OX = place("OX", 0, [P, HEADS, 2 * S], F32R)
        at = HEADS * 2 * BLK
        QK = [place(f"QK{i}", at + i * 6 * BLK, [P, GROUPS, 2, S]) for i in range(2)]
        at += 12 * BLK
        VT = [place(f"VT{i}", at + i * 3 * BLK, [P, GROUPS, 2, P]) for i in range(2)]
        at += 6 * BLK
        vrow = place("vrow", at, [P, GROUPS, S])
        swap = place("swap", at + 3 * BLK, [P, 2, S])
        rope = place("rope", at + 5 * BLK, [P, 2, S])
        at += 7 * BLK
        sm = place("sm", at, [P, SC])
        pt = place("pt", at + SC * 4, [P, SC])
        mask = place("mask", at + 2 * SC * 4, [P, SC])
        at += 3 * SC * 4
        nmax = place("nmax", at, [P, 2])
        rsum = place("rsum", at + 32, [P, 2])
        rrec = place("rrec", at + 64, [P, 2])
        out_sb = [place(f"out_sb{t}", t * D * 4, [P, D]) for t in range(2)]
        Y = nc.alloc_sbuf_tensor_at("Y", [P, KT, S], F32, offset=x_at)

        acc = [ctx.enter_context(nc.psum_tensor(f"acc{i}", [P, 2, 2 * S], F32)) for i in range(2)]
        sc_ps = ctx.enter_context(nc.psum_tensor("sc_ps", [P, 3, 512], F32))
        sc_flat = sc_ps[:, :, :].rearrange("p b c -> p (b c)")
        misc = ctx.enter_context(nc.psum_tensor("misc", [P, 512], F32))
        turn_ps = [sc_ps[:, 0, 0:S], sc_ps[:, 1, 0:S]]
        mix_ps = [sc_ps[:, 2, 0:S], misc[:, 0:S]]
        out_ps = sc_ps[:, 0, 0:S]
        Q1 = 512
        score_parts = ((0, Q0, 0), (Q0, SC, Q1))

        turned = [[acc[0][:, 0, :], acc[0][:, 1, :]], [sc_ps[:, 0, :], sc_ps[:, 1, :]],
                  [sc_ps[:, 2, :], misc[:, :]], [acc[1][:, 0, :], acc[1][:, 1, :]]]
        fin_ms = acc[1][:, 1, 0:2]

        def fin_turns(c, t):
            return 2 * c + t + 1

        raw_landed = [sem(f"raw_landed{i}") for i in range(RING)]
        vecs_landed = sem("vecs_landed")
        x_landed = [sem(f"x_landed{i}") for i in range(len(X_LOADS))]
        ws_landed = sem("ws_landed")
        bs_landed = sem("bs_landed")
        mask_landed = sem("mask_landed")
        rope_landed = sem("rope_landed")
        out_written = sem("out_written")
        hi_ready = sem("hi_ready")
        lo_ready = sem("lo_ready")
        units_done = sem("units_done")
        cleared = sem("cleared")
        ident_set = sem("ident_set")
        ws_masked = sem("ws_masked")
        hcopied = sem("hcopied")
        pair_summed = sem("pair_summed")
        half_added = sem("half_added")
        pair_taken = sem("pair_taken")
        x_hi = sem("x_hi")
        x_ready = sem("x_ready")
        x_squared = sem("x_squared")
        squared = sem("squared")
        ss_clear = sem("ss_clear")
        ss_added = sem("ss_added")
        ms_ready = sem("ms_ready")
        rms_ready = sem("rms_ready")
        rinv_ready = sem("rinv_ready")
        gelued = sem("gelued")
        v_added = sem("v_added")
        mean_ready = sem("mean_ready")
        centered = sem("centered")
        vss_clear = sem("vss_clear")
        ln_squared = sem("ln_squared")
        ln_added = sem("ln_added")
        var_ready = sem("var_ready")
        ln_std = sem("ln_std")
        ln_rinv_ready = sem("ln_rinv_ready")
        vn_scaled = sem("vn_scaled")
        vn_ready = sem("vn_ready")
        vn_turned = sem("vn_turned")
        vt_ready = sem("vt_ready")
        mixed = sem("mixed")
        mix_ready = sem("mix_ready")
        gated = sem("gated")
        gx_hi = sem("gx_hi")
        gx_ready = sem("gx_ready")
        tap2 = sem("tap2")
        tap1 = sem("tap1")
        tap0 = sem("tap0")
        silued = sem("silued")
        hid_made = sem("hid_made")
        hid_hi = sem("hid_hi")
        hid_ready = sem("hid_ready")
        swapped = sem("swapped")
        rope_sin = sem("rope_sin")
        rope_cos = sem("rope_cos")
        roped = sem("roped")
        swap_clear = sem("swap_clear")
        vh_turned = sem("vh_turned")
        vh_ready = sem("vh_ready")
        scored = sem("scored")
        masked = sem("masked")
        maxed = sem("maxed")
        exped = sem("exped")
        rsum_inv = sem("rsum_inv")
        normed = sem("normed")
        p_turned = sem("p_turned")
        pt_ready = sem("pt_ready")
        attended = sem("attended")
        o_hi = sem("o_hi")
        o_ready = sem("o_ready")
        y_ready = sem("y_ready")
        y_turned = sem("y_turned")
        y_done = [sem(f"y_done{t}") for t in range(2)]
        fin_rms = sem("fin_rms")
        fin_rinv_ready = sem("fin_rinv_ready")

        def vec(c):
            return vecs[:, c:c + 1]

        def over(ap, n):
            return ap[:, None, :].broadcast_to([P, n, S])

        block = ctx.enter_context(nc.Block())

        @block.sync
        def _(sp):
            def load(u, q, slot):
                sp.dma_start(raw[slot][:, :], w_stream[u, :, :]).then_inc(raw_landed[slot], 16)

            sp.dma_start(vecs[:, :], vecs_d).then_inc(vecs_landed, 16)
            for slot in range(RING):
                if slot:
                    sp.wait_ge(x_landed[slot + 1], 16)
                load(slot, 0, slot)
            with sp.Fori(1, UNITS // RING) as q:
                for slot in range(RING):
                    sp.wait_ge(lo_ready, RING * q + (slot + 1 - RING))
                    load(RING * q + slot, q, slot)
            for c in range(4):
                for t in range(2):
                    sp.wait_ge(y_done[t], c + 1)
                    sp.dma_start(out[P * t:P * (t + 1), 512 * c:512 * (c + 1)], out_sb[t][:, 512 * c:512 * (c + 1)])\
                        .then_inc(out_written, 16)
            sp.wait_ge(out_written, 8 * 16)

        @block.gpsimd
        def _(pool):
            nc.gpsimd.memset(mean_w[:, :], 1.0 / D).then_inc(cleared, 1)
            nc.gpsimd.memset(eps[:, :], EPS).then_inc(cleared, 1)
            nc.gpsimd.memset(gu[:, :, 0:2], 0.0).then_inc(cleared, 1)
            nc.gpsimd.memset(vsum[:, :, :], 0.0).then_inc(cleared, 1)
            nc.gpsimd.memset(ident[:, :], 0.0).then_inc(cleared, 1)
            pool.wait_ge(cleared, 5)
            nc.gpsimd.affine_select(out=ident[:, :], in_=ident[:, :], compare_op=ALU.not_equal, fill=1.0,
                                    base=0, pattern=[[-1, P]], channel_multiplier=1).then_inc(ident_set, 1)

            def norm_sums(n, pairs):
                pool.wait_ge(ms_ready, n)
                nc.gpsimd.memset(ssum[:, :], 0.0).then_inc(ss_clear, 1)
                pool.wait_ge(ss_clear, n + 1)
                with pool.Fori(0, pairs) as i:
                    pool.wait_ge(squared, pairs * (n - 1) + POOL_PAIRS + 1 + i)
                    pool.wait_ge(ss_added, pairs * n + i)
                    nc.gpsimd.tensor_tensor(ssum[:, :], ssum[:, :], sq[:, :, :].rearrange("p a b -> p (a b)"),
                                            ALU.add).then_inc(ss_added, 1)

            nc.gpsimd.memset(ssum[:, :], 0.0).then_inc(ss_clear, 1)
            pool.wait_ge(ss_clear, 1)
            for i in range(NORM_PAIRS):
                if i < POOL_PAIRS:
                    pool.wait_ge(x_landed[X_PAIRS[i]], 16)
                    wait_pos(pool, ss_added, i)
                    nc.gpsimd.tensor_tensor(sq[:, :, :], h[:, pair_of(i), :], h[:, pair_of(i), :], ALU.mult)\
                        .then_inc(squared, 1)
                    pool.wait_ge(squared, i + 1)
                else:
                    pool.wait_ge(x_squared, i - POOL_PAIRS + 1)
                    pool.wait_ge(ss_added, i)
                source = sq if i < POOL_PAIRS else (tsum, hc)[i % 2]
                nc.gpsimd.tensor_tensor(ssum[:, :], ssum[:, :], source[:, :, :].rearrange("p a b -> p (a b)"),
                                        ALU.add).then_inc(ss_added, 1)
            pool.dma_start(WS[:, :, :], ws_t).then_inc(ws_landed, 16)
            pool.dma_start(BS[:, :, :].rearrange("p a b -> p (a b)"), bs_row.partition_broadcast(P))\
                .then_inc(bs_landed, 16)
            pool.wait_ge(ws_landed, 16)
            nc.gpsimd.affine_select(out=WS[:, :, :], in_=WS[:, :, :], compare_op=ALU.is_ge, fill=0.0,
                                    base=0, pattern=[[0, KT], [1, P]], channel_multiplier=-1).then_inc(ws_masked, 1)
            for p in range(KT // 2):
                pool.wait_ge(gelued, p + 1)
                if p:
                    pool.wait_ge(v_added, p)
                nc.gpsimd.tensor_tensor(vsum[:, :, :], vsum[:, :, :], V[:, 2 * p:2 * p + 2, :], ALU.add)\
                    .then_inc(v_added, 1)
            pool.wait_ge(mean_ready, 1)
            nc.gpsimd.memset(vsum[:, :, :], 0.0).then_inc(vss_clear, 1)
            pool.wait_ge(vss_clear, 1)
            for c in range(4):
                pool.wait_ge(ln_squared, c + 1)
                for k in range(2):
                    if c or k:
                        pool.wait_ge(ln_added, 2 * c + k)
                    nc.gpsimd.tensor_tensor(vsum[:, :, :], vsum[:, :, :], U[:, 12 + 2 * k:14 + 2 * k, :], ALU.add)\
                        .then_inc(ln_added, 1)
            for j in range(KT // 2 - 1):
                pool.wait_ge(gelued, P_U + j + 1)
                pool.wait_ge(mix_ready, 2 * j + 2)
                nc.gpsimd.tensor_tensor(U[:, 2 * j:2 * j + 2, :], U[:, 2 * j:2 * j + 2, :],
                                        V[:, 2 * j:2 * j + 2, :], ALU.mult).then_inc(gated, 1)
            norm_sums(1, KT // 2)
            norm_sums(2, KT // 2)
            pool.wait_ge(units_done, U_QKV)
            pool.dma_start(rope[:, :, :], rope_d).then_inc(rope_landed, 16)
            pool.dma_start(mask[:, :], mask_d).then_inc(mask_landed, 16)
            nc.gpsimd.memset(swap[:, :, :], 0.0).then_inc(swap_clear, 1)
            norm_sums(3, KT // 2)
            pool.wait_ge(ms_ready, 4)
            nc.gpsimd.memset(ssum[:, :], 0.0).then_inc(ss_clear, 1)
            pool.wait_ge(ss_clear, 5)
            for i in range(NORM_PAIRS):
                n = 2 if i < NORM_PAIRS - 1 else 1
                pool.wait_ge(squared, NORM_PAIRS * 3 + POOL_PAIRS + 1 + i)
                pool.wait_ge(ss_added, NORM_PAIRS * 4 + i)
                nc.gpsimd.tensor_tensor(ssum[:, 0:S * n], ssum[:, 0:S * n],
                                        sq[:, 0:n, :].rearrange("p a b -> p (a b)"), ALU.add).then_inc(ss_added, 1)

        @block.scalar
        def _(act):
            def split_step(first, s, rounds=0):
                c = first + s + AHEAD
                slot, q = c % RING, rounds + c // RING
                act.wait_ge(raw_landed[slot], 16 * q + 16)
                wait_pos(act, units_done, RING * rounds + (c + 1 - RING))
                nc.scalar.activation(w_hi[slot][:, :], raw[slot][:, :], ACT.Copy).then_inc(hi_ready, 1)

            def settled():
                act.wait_ge(vecs_landed, 16)

            def high_copy(pair, s, done):
                act.wait_ge(units_done, done)
                nc.scalar.activation(hc[:, :, :], acc[s][:, :, 0:S], ACT.Copy).then_inc(hcopied, 1)

            def square_pair(pr):
                nc.scalar.activation(sq[:, :, :], h[:, pair_of(pr), :], ACT.Square).then_inc(squared, 1)

            def norm_pair(n, pr):
                wait_pos(act, ss_added, NORM_PAIRS * n + pr)
                settled()
                for b in range(2):
                    nc.scalar.activation(X[:, 2 * pr + b, 0:S], h[:, 2 * pr + b, :], ACT.Copy,
                                         scale=vecs[:, one(GAINS[n] + 2 * pr + b)]).then_inc(x_hi, 1)
                square_pair(pr)

            def rms(n):
                act.wait_ge(ms_ready, n + 1)
                act.wait_ge(cleared, 5)
                nc.scalar.activation(std[:, :], misc[:, 0:S], ACT.Sqrt, bias=eps[:, :]).then_inc(rms_ready, 1)

            def gelu_evac(pair, pr, stage, s, dst, done):
                if stage == 0:
                    high_copy(pair, s, done)
                if stage == 1:
                    act.wait_ge(pair_taken, pair + 1)
                    settled()
                    nc.scalar.activation(dst[:, pair_of(pr), :], gu[:, :, 2:S + 2], ACT.Gelu_apprx_tanh)\
                        .then_inc(gelued, 1)

            def residual(n, pair, pr):
                act.wait_ge(pair_summed, pair + 1)
                if n < 4:
                    norm_pair(n, pr)
                else:
                    act.wait_ge(ss_added, NORM_PAIRS * n + pr)
                    for b in range(2):
                        nc.scalar.activation(Y[:, 2 * pr + b, :], h[:, 2 * pr + b, :], ACT.Copy,
                                             scale=vec(C_FIN + 2 * pr + b)).then_inc(y_ready, 1)
                    square_pair(pr)

            def last_block(b):
                act.wait_ge(pair_summed, P_D1 + KT // 2 + b)
                if b == 0:
                    act.wait_ge(ss_added, NORM_PAIRS * 5 - 1)
                kt = KT - 2 + b
                nc.scalar.activation(sq[:, b, :], h[:, kt, :], ACT.Square).then_inc(squared, 1)
                nc.scalar.activation(Y[:, kt, :], h[:, kt, :], ACT.Copy, scale=vec(C_FIN + kt)).then_inc(y_ready, 1)

            def ffn_evac(layer, pair, j, stage, s, done):
                f = FB * layer + j
                cv = C_CONV + 4 * FB * layer
                taken = pair + 1 - (ADDED_F1 if layer else ADDED_F0)
                if stage == 0:
                    high_copy(pair, s, done)
                if stage == 1:
                    act.wait_ge(pair_taken, taken)
                    settled()
                    nc.scalar.activation(conv[:, :], gu[:, 0, 2:S + 2], ACT.Identity,
                                         bias=vecs[:, one(cv + 3 * FB + j)],
                                         scale=vecs[:, one(cv + 2 * FB + j)]).then_inc(tap2, 1)
                if stage == 2:
                    act.wait_ge(tap0, f + 1)
                    nc.scalar.activation(act_g[:, :], conv[:, :], ACT.Silu).then_inc(silued, 1)
                if stage == 3:
                    act.wait_ge(hid_made, f + 1)
                    settled()
                    nc.scalar.activation(hid[:, j, 0:S], hidden[:, :], ACT.Copy).then_inc(hid_hi, 1)

            def ffn(layer, u0, p0, ud, pd):
                rms(1 + 2 * layer)
                with act.Fori(0, FB // 2) as i:
                    for s in range(4, 12):
                        c = s // 4 - 1
                        split_step(u0, s, rounds=2 * i)
                        ffn_evac(layer, p0 + 2 * i + c, 2 * i + c, s % 4, c, u0 + 8 * i + 4 * (c + 1))

                def down(i, s):
                    c = s // 11 - 1
                    if ud + 44 + s + AHEAD < UNITS or layer == 0 or i == 0:
                        split_step(ud, s, rounds=11 * i)
                    if c >= 0 and s % 11 == 0:
                        residual(2 + 2 * layer, pd + 4 * i + c, 4 * i + c)

                if layer == 0:
                    with act.Fori(0, 2) as i:
                        for s in range(4, 48):
                            down(i, s)
                else:
                    for s in range(4, 48):
                        down(0, s)
                    nc.scalar.activation(std[:, 0:1], eps[:, :], ACT.Sqrt).then_inc(rms_ready, 1)
                    for s in range(4, 44):
                        down(1, s)
                        if s == 39:
                            last_block(0)
                    last_block(1)

            at = 0
            for load, n in enumerate(X_LOADS):
                act.dma_start(h[:, at:at + n, :], x_t[:, at:at + n, :]).then_inc(x_landed[load], 16)
                at += n
            act.wait_ge(cleared, 5)
            nc.scalar.activation(std[:, 0:1], eps[:, :], ACT.Copy).then_inc(rms_ready, 1)
            act.wait_ge(vecs_landed, 16)
            b = 0
            for load, n in enumerate(X_LOADS):
                act.wait_ge(x_landed[load], 16)
                if load == 1:
                    split_step(U_V, -2)
                for _ in range(n):
                    nc.scalar.activation(X[:, b, 0:S], h[:, b, :], ACT.Copy, scale=vec(GAINS[0] + b)).then_inc(x_hi, 1)
                    b += 1
                if load == 3:
                    split_step(U_V, -1)
            for s in range(4):
                i = POOL_PAIRS + s
                wait_pos(act, ss_added, i - 1 if s >= 2 else 0)
                nc.scalar.activation((tsum, hc)[i % 2][:, :, :], h[:, pair_of(i), :], ACT.Square).then_inc(x_squared, 1)
                split_step(U_V, s)
            rms(0)
            with act.Fori(0, KT // 4) as i:
                for s in range(4, 12):
                    c = s // 4 - 1
                    split_step(U_V, s, rounds=2 * i)
                    gelu_evac(P_V + 2 * i + c, 2 * i + c, s % 4, c, V, U_V + 8 * i + 4 * (c + 1))
            for k in range(4, KT * KT // UT + 4):
                split_step(U_U, k)
                j = k // 4 - 1
                if j == 6 and k % 4 == 1:
                    act.wait_ge(ln_added, 8)
                gelu_evac(P_U + j, j, k % 4, j % 2, U, U_U + 4 * (j + 1))
                if 5 <= k < 9:
                    c = k - 5
                    act.wait_ge(centered, c + 1)
                    wait_pos(act, ln_added, 2 * c)
                    nc.scalar.activation(U[:, 12:16, :], V[:, 4 * c:4 * c + 4, :], ACT.Square).then_inc(ln_squared, 1)
                if k == 10:
                    act.wait_ge(var_ready, 1)
                    nc.scalar.activation(std[:, :], misc[:, S:2 * S], ACT.Sqrt, bias=eps[:, :]).then_inc(ln_std, 1)
                g = k - 15
                if 0 <= g < KT:
                    act.wait_ge(vn_turned, g + 1)
                    wait_pos(act, mixed, g - 1)
                    nc.scalar.activation(vt[g % 2][:, :, :].rearrange("p a b -> p (a b)"),
                                         turn_ps[g % 2], ACT.Copy).then_inc(vt_ready, 1)
                for jg in range(NORM_PAIRS):
                    if k == gx_step(jg):
                        act.wait_ge(gated, jg + 1)
                        nc.scalar.activation(GX[:, pair_of(jg), 0:S], U[:, pair_of(jg), :], ACT.Copy).then_inc(gx_hi, 1)
            with act.Fori(0, KT // 4) as i:
                for s in range(4, 12):
                    c = s // 4 - 1
                    split_step(U_AO, s, rounds=2 * i)
                    if s % 4 == 0:
                        residual(1, P_AO + 2 * i + c, 2 * i + c)
            ffn(0, U_F0, P_F0, U_D0, P_D0)

            def evac(h_, m, stage, par):
                pair = P_QKV + HEAD_PAIRS * h_ + m
                if stage == 0:
                    act.wait_ge(units_done, U_QKV + HEAD_UNITS * h_ + (4 * (m + 1) if m < 4 else HEAD_UNITS))
                    act.wait_ge(pair_summed, pair)
                    n = 2 if m < 4 else 1
                    nc.scalar.activation(hc[:, 0:n, :], acc[(par + m) % 2][:, 0:n, 0:S], ACT.Copy).then_inc(hcopied, 1)
                if stage == 1 and m < GROUPS:
                    gi = GROUPS * h_ + m
                    act.wait_ge(pair_taken, pair + 1 - ADDED_QKV)
                    act.wait_ge(swap_clear, 1)
                    wait_pos(act, roped, gi)
                    nc.scalar.activation(swap[0:HALF, :, :], QK[par][2 * HALF:3 * HALF, m, :, :], ACT.Copy)\
                        .then_inc(swapped, 1)
                    nc.scalar.activation(swap[2 * HALF:3 * HALF, :, :], QK[par][0:HALF, m, :, :], ACT.Copy)\
                        .then_inc(swapped, 1)

            def v_turn(h_, part, par):
                act.wait_ge(vh_turned, 2 * h_ + part + 1)
                a, b = ((0, 2), (2, 3))[part]
                nc.scalar.activation(VT[par][:, a:b, :, :].rearrange("p g a b -> p (g a b)"),
                                     misc[:, 0:S * (b - a)], ACT.Copy).then_inc(vh_ready, 1)

            def softmax_exp(h_):
                for t, (a, b, _) in enumerate(score_parts):
                    act.wait_ge(maxed, 2 * h_ + t + 1)
                    nc.scalar.activation(sm[:, a:b], sm[:, a:b], ACT.Exp, bias=nmax[:, t:t + 1],
                                         accum_out=rsum[:, t:t + 1]).then_inc(exped, 1)

            def p_turn(h_):
                act.wait_ge(p_turned, h_ + 1)
                for a, b, c in score_parts:
                    nc.scalar.activation(pt[:, a:b], sc_flat[:, c:c + b - a], ACT.Copy).then_inc(pt_ready, 1)

            def head_out(h_):
                act.wait_ge(attended, h_ + 1)
                settled()
                nc.scalar.activation(OX[:, h_, 0:S], out_ps, ACT.Copy).then_inc(o_hi, 1)

            def head_step(h_, par, t, before, rounds=0, c0=0):
                split_step(U_QKV + c0, t, rounds=rounds)
                if before:
                    if t < 1:
                        evac(h_ - 1, 4, 0, 1 - par)
                        v_turn(h_ - 1, 0, 1 - par)
                    if t == 2:
                        v_turn(h_ - 1, 1, 1 - par)
                        p_turn(h_ - 1)
                    if t == 6:
                        head_out(h_ - 1)
                if t >= 4:
                    evac(h_, t // 4 - 1, t % 4, par)
                if t == 16:
                    softmax_exp(h_)

            rms(2)
            for t in range(4, HEAD_UNITS):
                head_step(0, 0, t, False)
            with act.Fori(0, 3) as i:
                for k in range(2):
                    for t in range(HEAD_UNITS):
                        head_step(2 * i + 1 + k, 1 - k, t, True, rounds=9 * i, c0=HEAD_UNITS * (1 + k))
            last = HEADS - 1
            for t in range(HEAD_UNITS):
                head_step(last, 1, t, True, c0=HEAD_UNITS * last)
            split_step(U_WO, 0)
            evac(last, 4, 0, 1)
            v_turn(last, 0, 1)
            split_step(U_WO, 1)
            p_turn(last)
            v_turn(last, 1, 1)
            head_out(last)
            with act.Fori(0, 4) as i:
                for s in range(2, 6):
                    c = s // 2 - 1
                    split_step(U_WO, s, rounds=i)
                    if s % 2:
                        residual(3, P_WO + 2 * i + c, 2 * i + c)
            for s in range(2, 4):
                split_step(U_F1, s)
            ffn(1, U_F1, P_F1, U_D1, P_D1)
            act.wait_ge(ms_ready, 5)
            nc.scalar.activation(fin_std[:, :], fin_ms, ACT.Sqrt, bias=eps[:, :]).then_inc(fin_rms, 1)
            act.wait_ge(fin_rinv_ready, 1)
            for c in range(4):
                act.wait_ge(y_turned, fin_turns(c, 1))
                nc.scalar.activation(out_sb[1][:, 512 * c:512 * (c + 1)], turned[c][1], ACT.Copy,
                                     scale=fin_rinv[:, 1:2]).then_inc(y_done[1], 1)

        @block.vector
        def _(dve):
            def split_step(first, s, rounds=0):
                c = first + s + AHEAD
                slot = c % RING
                dve.wait_ge(hi_ready, RING * rounds + c + 1)
                nc.vector.tensor_tensor(w_lo[slot][:, :], raw[slot][:, :], w_hi[slot][:, :], ALU.subtract)\
                    .then_inc(lo_ready, 1)

            def sum_pair(pair, s, added):
                dve.wait_ge(hcopied, pair + 1 - added)
                nc.vector.tensor_tensor(tsum[:, :, :], hc[:, :, :], acc[s][:, :, S:2 * S], ALU.add)\
                    .then_inc(pair_summed, 1)

            def inverse_rms(n):
                dve.wait_ge(rms_ready, n + 2)
                nc.vector.reciprocal(rinv[:, :], std[:, :]).then_inc(rinv_ready, 1)
                dve.wait_ge(rinv_ready, n + 1)

            def x_low(n, pr):
                for b in range(2):
                    dve.wait_ge(x_hi, KT * n + 2 * pr + b + 1)
                    nc.vector.scalar_tensor_tensor(X[:, 2 * pr + b, S:2 * S], h[:, 2 * pr + b, :],
                                                   vecs[:, one(GAINS[n] + 2 * pr + b)], X[:, 2 * pr + b, 0:S],
                                                   ALU.mult, ALU.subtract).then_inc(x_ready, 1)

            def scale_pair(pair, s, added=0):
                sum_pair(pair, s, added)
                dve.wait_ge(pair_summed, pair + 1)
                nc.vector.tensor_tensor(gu[:, :, 2:S + 2], tsum[:, :, :], over(rinv, 2), ALU.mult)\
                    .then_inc(pair_taken, 1)

            def add_to_h(blocks_, source, done, summed, halves):
                dve.wait_ge(units_done, done)
                to = tsum[:, 0:source.shape[1], :]
                nc.vector.tensor_tensor(to, h[:, blocks_, :], source[:, :, 0:S], ALU.add).then_inc(half_added, 1)
                dve.wait_ge(half_added, halves + 1)
                nc.vector.tensor_tensor(h[:, blocks_, :], to, source[:, :, S:2 * S], ALU.add).then_inc(pair_summed, 1)

            def residual(n, pair, pr, s, done):
                add_to_h(pair_of(pr), acc[s][:, :, :], done, pair, NORM_PAIRS * (n - 1) + pr)

            def ffn_evac(layer, pair, j, stage, s):
                f = FB * layer + j
                cv = C_CONV + 4 * FB * layer
                if stage == 0:
                    scale_pair(pair, s, ADDED_F1 if layer else ADDED_F0)
                if stage == 1:
                    dve.wait_ge(tap2, f + 1)
                    nc.vector.scalar_tensor_tensor(conv[:, :], gu[:, 0, 1:S + 1], vecs[:, one(cv + FB + j)], conv[:, :],
                                                   ALU.mult, ALU.add).then_inc(tap1, 1)
                    dve.wait_ge(tap1, f + 1)
                    nc.vector.scalar_tensor_tensor(conv[:, :], gu[:, 0, 0:S], vecs[:, one(cv + j)], conv[:, :],
                                                   ALU.mult, ALU.add).then_inc(tap0, 1)
                if stage == 2:
                    dve.wait_ge(silued, f + 1)
                    dve.wait_ge(hid_ready, f + 1)
                    nc.vector.tensor_tensor(hidden[:, :], act_g[:, :], gu[:, 1, 2:S + 2], ALU.mult)\
                        .then_inc(hid_made, 1)
                if stage == 3:
                    dve.wait_ge(hid_hi, f + 1)
                    nc.vector.tensor_tensor(hid[:, j, S:2 * S], hidden[:, :], hid[:, j, 0:S], ALU.subtract)\
                        .then_inc(hid_ready, 1)

            def ffn(layer, u0, p0, ud, pd):
                inverse_rms(1 + 2 * layer)
                with dve.Fori(0, FB // 2) as i:
                    for s in range(4, 12):
                        c = s // 4 - 1
                        split_step(u0, s, rounds=2 * i)
                        ffn_evac(layer, p0 + 2 * i + c, 2 * i + c, s % 4, c)

                def down(i, s):
                    c = s // 11 - 1
                    if ud + 44 + s + AHEAD < UNITS or layer == 0 or i == 0:
                        split_step(ud, s, rounds=11 * i)
                    if c >= 0 and s % 11 == 0:
                        residual(2 + 2 * layer, pd + 4 * i + c, 4 * i + c, c % 2, ud + 44 * i + 11 * (c + 1))
                        if layer == 0:
                            x_low(2, 4 * i + c)

                if layer == 0:
                    with dve.Fori(0, 2) as i:
                        for s in range(4, 48):
                            down(i, s)
                else:
                    for s in range(4, 48):
                        down(0, s)
                    for s in range(4, 44):
                        down(1, s)
                        if s == 39:
                            last_block(0)
                    last_block(1)

            def last_block(b):
                add_to_h(slice(KT - 2 + b, KT - 1 + b), acc[1][:, b:b + 1, :], UNITS - 5 if b == 0 else UNITS,
                         P_D1 + KT // 2 - 1 + b, NORM_PAIRS * 4 - 1 + b)

            nc.vector.memset(hidden[:, :], 0.0).then_inc(hid_ready, 1)
            dve.wait_ge(vecs_landed, 16)
            split_step(U_V, -2)
            for pr in range(NORM_PAIRS):
                x_low(0, pr)
                if pr == 5:
                    split_step(U_V, -1)
            for s in range(4):
                split_step(U_V, s)
            inverse_rms(0)
            with dve.Fori(0, KT // 4) as i:
                for s in range(4, 12):
                    c = s // 4 - 1
                    split_step(U_V, s, rounds=2 * i)
                    if s % 4 == 0:
                        scale_pair(P_V + 2 * i + c, c)
            def mix_bias(g):
                dve.wait_ge(mixed, g + 1)
                if g == 0:
                    dve.wait_ge(bs_landed, 16)
                nc.vector.tensor_tensor(V[:, g, :].rearrange("p (n t) -> p n t", n=2),
                                        mix_ps[g % 2].rearrange("p (n t) -> p n t", n=2),
                                        BS[:, g, None, :].broadcast_to([P, 2, P]), ALU.add).then_inc(mix_ready, 1)

            def gx_low(jg):
                dve.wait_ge(gx_hi, jg + 1)
                nc.vector.tensor_tensor(GX[:, pair_of(jg), S:2 * S], U[:, pair_of(jg), :],
                                        GX[:, pair_of(jg), 0:S], ALU.subtract).then_inc(gx_ready, 1)

            for k in range(4, KT * KT // UT + 4):
                j = k // 4 - 1
                if k == 32:
                    mix_bias(KT - 1)
                    scale_pair(P_U + j, j % 2)
                if k == 33:
                    dve.wait_ge(gelued, P_U + NORM_PAIRS)
                    dve.wait_ge(mix_ready, KT)
                    nc.vector.tensor_tensor(U[:, KT - 2:, :], U[:, KT - 2:, :], V[:, KT - 2:, :], ALU.mult)\
                        .then_inc(gated, 1)
                    gx_low(NORM_PAIRS - 1)
                split_step(U_U, k)
                if k % 4 == 0 and k < 32:
                    scale_pair(P_U + j, j % 2)
                if 4 <= k < 8:
                    c = k - 4
                    dve.wait_ge(mean_ready, 1)
                    nc.vector.tensor_tensor(V[:, 4 * c:4 * c + 4, :], V[:, 4 * c:4 * c + 4, :],
                                            over(misc[:, 0:S], 4), ALU.subtract).then_inc(centered, 1)
                if k == 11:
                    dve.wait_ge(ln_std, 1)
                    nc.vector.reciprocal(ln_rinv[:, :], std[:, :]).then_inc(ln_rinv_ready, 1)
                    dve.wait_ge(ln_rinv_ready, 1)
                g = k - 12
                if 0 <= g < KT:
                    wait_pos(dve, vn_turned, g - 1)
                    nc.vector.scalar_tensor_tensor(vn[g % 2][:, :], V[:, g, :], vec(C_SG + g), ln_rinv[:, :],
                                                   ALU.mult, ALU.mult).then_inc(vn_scaled, 1)
                    dve.wait_ge(vn_scaled, g + 1)
                    nc.vector.tensor_scalar(vn[g % 2][:, :], vn[g % 2][:, :], vec(C_SB + g), None, ALU.add)\
                        .then_inc(vn_ready, 1)
                g = k - 17
                if 0 <= g < KT - 1:
                    mix_bias(g)
                for jg in range(NORM_PAIRS - 1):
                    if k == gx_step(jg):
                        gx_low(jg)
            with dve.Fori(0, KT // 4) as i:
                for s in range(4, 12):
                    c = s // 4 - 1
                    split_step(U_AO, s, rounds=2 * i)
                    if s % 4 == 0:
                        residual(1, P_AO + 2 * i + c, 2 * i + c, c, U_AO + 8 * i + 4 * (c + 1))
                        x_low(1, 2 * i + c)
            ffn(0, U_F0, P_F0, U_D0, P_D0)

            def evac(h_, m, stage, par):
                pair = P_QKV + HEAD_PAIRS * h_ + m
                if stage == 0:
                    n = 2 if m < 4 else 1
                    dve.wait_ge(hcopied, pair + 1 - ADDED_QKV)
                    nc.vector.tensor_tensor(tsum[:, 0:n, :], hc[:, 0:n, :], acc[(par + m) % 2][:, 0:n, S:2 * S], ALU.add)\
                        .then_inc(pair_summed, 1)
                    dve.wait_ge(pair_summed, pair + 1)
                    to = QK[par][:, m, :, :] if m < GROUPS else vrow[:, 2 * (m - 3):2 * (m - 3) + n, :]
                    nc.vector.tensor_tensor(to, tsum[:, 0:n, :], over(rinv, n), ALU.mult).then_inc(pair_taken, 1)
                if stage == 1 and m < GROUPS:
                    gi = GROUPS * h_ + m
                    rows = 3 * HALF
                    dve.wait_ge(rope_landed, 16)
                    dve.wait_ge(swapped, 2 * gi + 2)
                    nc.vector.tensor_tensor(swap[0:rows, :, :], swap[0:rows, :, :],
                                            rope[0:rows, 1, None, :].broadcast_to([rows, 2, S]), ALU.mult)\
                        .then_inc(rope_sin, 1)
                    nc.vector.tensor_tensor(QK[par][0:rows, m, :, :], QK[par][0:rows, m, :, :],
                                            rope[0:rows, 0, None, :].broadcast_to([rows, 2, S]), ALU.mult)\
                        .then_inc(rope_cos, 1)
                    dve.wait_ge(rope_sin, gi + 1)
                    dve.wait_ge(rope_cos, gi + 1)
                    nc.vector.tensor_tensor(QK[par][0:rows, m, :, :], QK[par][0:rows, m, :, :], swap[0:rows, :, :],
                                            ALU.add).then_inc(roped, 1)

            def mask_scores(h_):
                dve.wait_ge(mask_landed, 16)
                dve.wait_ge(scored, h_ + 1)
                for a, b, c in score_parts:
                    nc.vector.scalar_tensor_tensor(sm[:, a:b], sc_flat[:, c:c + b - a], float(E) ** -0.5, mask[:, a:b],
                                                   ALU.mult, ALU.add).then_inc(masked, 1)
                for t, (a, b, _) in enumerate(score_parts):
                    dve.wait_ge(masked, 2 * h_ + t + 1)
                    nc.vector.reduce_max(nmax[:, t:t + 1], sm[:, a:b], AX_X, negate=True).then_inc(maxed, 1)

            def normalize(h_):
                dve.wait_ge(exped, 2 * h_ + 2)
                nc.vector.reciprocal(rrec[:, :], rsum[:, :]).then_inc(rsum_inv, 1)
                dve.wait_ge(rsum_inv, h_ + 1)
                for t, (a, b, _) in enumerate(score_parts):
                    nc.vector.tensor_scalar(sm[:, a:b], sm[:, a:b], rrec[:, t:t + 1], None, ALU.mult)\
                        .then_inc(normed, 1)

            def head_out(h_):
                dve.wait_ge(o_hi, h_ + 1)
                nc.vector.tensor_tensor(OX[:, h_, S:2 * S], out_ps, OX[:, h_, 0:S], ALU.subtract)\
                    .then_inc(o_ready, 1)

            def head_step(h_, par, t, before, rounds=0, c0=0):
                split_step(U_QKV + c0, t, rounds=rounds)
                if before and t == 0:
                    evac(h_ - 1, 4, 0, 1 - par)
                if before and t == 6:
                    head_out(h_ - 1)
                if t >= 4:
                    evac(h_, t // 4 - 1, t % 4, par)
                if t == 15:
                    mask_scores(h_)
                if t == 17:
                    normalize(h_)

            inverse_rms(2)
            for t in range(4, HEAD_UNITS):
                head_step(0, 0, t, False)
            with dve.Fori(0, 3) as i:
                for k in range(2):
                    for t in range(HEAD_UNITS):
                        head_step(2 * i + 1 + k, 1 - k, t, True, rounds=9 * i, c0=HEAD_UNITS * (1 + k))
            last = HEADS - 1
            for t in range(HEAD_UNITS):
                head_step(last, 1, t, True, c0=HEAD_UNITS * last)
            split_step(U_WO, 0)
            evac(last, 4, 0, 1)
            split_step(U_WO, 1)
            head_out(last)
            with dve.Fori(0, 4) as i:
                for s in range(2, 6):
                    c = s // 2 - 1
                    if s % 2 == 0:
                        residual(3, P_WO + 2 * i + c, 2 * i + c, c, U_WO + 4 * i + 2 * (c + 1))
                    split_step(U_WO, s, rounds=i)
                    if s % 2:
                        x_low(3, 2 * i + c)
            for s in range(2, 4):
                split_step(U_F1, s)
            ffn(1, U_F1, P_F1, U_D1, P_D1)
            dve.wait_ge(fin_rms, 1)
            nc.vector.reciprocal(fin_rinv[:, :], fin_std[:, :]).then_inc(fin_rinv_ready, 1)
            dve.wait_ge(fin_rinv_ready, 1)
            for c in range(4):
                dve.wait_ge(y_turned, fin_turns(c, 0))
                nc.vector.tensor_scalar(out_sb[0][:, 512 * c:512 * (c + 1)], turned[c][0], fin_rinv[:, 0:1], None,
                                        ALU.mult).then_inc(y_done[0], 1)

        @block.tensor
        def _(pe):
            def multiply(u, slot, tiles, needs=None):
                pe.wait_ge(lo_ready, u + 1)
                for n, (bank, moving, kt, first, last) in enumerate(tiles):
                    if needs:
                        needs(kt)
                    hi = w_hi[slot][:, n * P:(n + 1) * P]
                    lo = w_lo[slot][:, n * P:(n + 1) * P]
                    if not last:
                        nc.tensor.matmul(bank, hi, moving[:, kt, :], start=first, stop=False)
                        op = nc.tensor.matmul(bank[:, S:2 * S], lo, moving[:, kt, 0:S], start=False, stop=False)
                    else:
                        nc.tensor.matmul(bank[:, S:2 * S], lo, moving[:, kt, 0:S], start=False, stop=False)
                        op = nc.tensor.matmul(bank, hi, moving[:, kt, :], start=False, stop=True)
                op.then_inc(units_done, 1)

            def tiles_of(pair_set, moving, k_tiles, n):
                at = [n * UT + t for t in range(UT)]
                return [(acc[pair_set][:, a // k_tiles, :], moving, a % k_tiles, a % k_tiles == 0,
                         a % k_tiles == k_tiles - 1) for a in at]

            def two_pairs(u, pair, moving, k_tiles, needs=None, after=None):
                per = 2 * k_tiles // UT
                for n in range(2 * per):
                    if n % per == 0:
                        wait_pos(pe, pair_summed, pair + n // per - 1)
                    multiply(u + n, n % RING, tiles_of(n // per, moving, k_tiles, n % per),
                             needs if n < k_tiles // UT else None)
                    if after:
                        after(n)

            def mean_square(n):
                pe.wait_ge(ss_added, NORM_PAIRS * (n + 1))
                for b in range(2):
                    op = nc.tensor.matmul(misc[:, 0:S], mean_w[:, :], ssum[:, b * S:(b + 1) * S],
                                          start=(b == 0), stop=(b == 1))
                op.then_inc(ms_ready, 1)

            def normed_ready(n):
                return lambda kt: pe.wait_ge(x_ready, KT * n + kt + 1)

            def product(u0, p0, pairs, moving, k_tiles, needs, n=None):
                two_pairs(u0, p0, moving, k_tiles, needs, (lambda k: mean_square(n) if k == 3 else None)
                          if n is not None else None)
                per = 4 * k_tiles // UT
                with pe.Fori(1, pairs // 2) as i:
                    two_pairs(u0 + per * i, p0 + 2 * i, moving, k_tiles)

            def down(layer, ud, pd):
                with pe.Fori(0, 2) as i:
                    pe.wait_ge(hid_ready, FB * (layer + 1))
                    for c in range(4):
                        wait_pos(pe, pair_summed, pd + 4 * i + c - 1)
                        for n in range(11):
                            def needs(kt, c=c, n=n):
                                if c == 0 and n < 6 and kt == FB - 1:
                                    pe.wait_ge(hid_ready, FB * (layer + 1) + 1)
                            multiply(ud + 44 * i + 11 * c + n, (11 * c + n) % RING, tiles_of(c % 2, hid, FB, n), needs)

            pe.wait_ge(cleared, 5)
            pe.wait_ge(ident_set, 1)
            product(U_V, P_V, KT // 2, X, KT, normed_ready(0), 0)

            for k in range(KT * KT // UT):
                if k % 4 == 0:
                    pe.wait_ge(pair_summed, P_U + k // 4 - 1)
                multiply(U_U + k, k % RING, tiles_of(k // 4 % 2, X, KT, k % 4))
                if k == 3:
                    pe.wait_ge(v_added, KT // 2)
                    for b in range(2):
                        op = nc.tensor.matmul(misc[:, 0:S], mean_w[:, :], vsum[:, b, :], start=(b == 0), stop=(b == 1))
                    op.then_inc(mean_ready, 1)
                if k == 10:
                    pe.wait_ge(ln_added, 8)
                    for b in range(2):
                        op = nc.tensor.matmul(misc[:, S:2 * S], mean_w[:, :], vsum[:, b, :], start=(b == 0), stop=(b == 1))
                    op.then_inc(var_ready, 1)
                g = k - 16
                if 0 <= g < KT:
                    pe.wait_ge(vt_ready, g + 1)
                    wait_pos(pe, mix_ready, g - 1)
                    pe.wait_ge(ws_masked, 1)
                    for n in range(2):
                        op = nc.tensor.matmul(mix_ps[g % 2][:, P * n:P * (n + 1)],
                                              vt[g % 2][:, n, :], WS[:, g, :], start=True, stop=True)
                    op.then_inc(mixed, 1)
                g = k - 14
                if 0 <= g < KT:
                    pe.wait_ge(vn_ready, g + 1)
                    wait_pos(pe, vt_ready, g - 1)
                    for n in range(2):
                        op = nc.tensor.transpose(turn_ps[g % 2][:, P * n:P * (n + 1)],
                                                 vn[g % 2][:, P * n:P * (n + 1)], ident[:, :])
                    op.then_inc(vn_turned, 1)

            def gx_needed(kt):
                if kt % 2 == 0:
                    pe.wait_ge(gx_ready, kt // 2 + 1)

            product(U_AO, P_AO, KT // 2, GX, KT, gx_needed)
            product(U_F0, P_F0, FB, X, KT, normed_ready(1), 1)
            down(0, U_D0, P_D0)

            def v_turn(h_, part):
                pe.wait_ge(pair_taken, P_QKV - ADDED_QKV + HEAD_PAIRS * h_ + 4 + part)
                if part:
                    pe.wait_ge(vh_ready, 2 * h_ + 1)
                a, b = ((0, 2), (2, 3))[part]
                for n in range(2 * (b - a)):
                    op = nc.tensor.transpose(misc[:, P * n:P * (n + 1)],
                                             vrow[:, a + n // 2, P * (n % 2):P * (n % 2 + 1)], ident[:, :])
                op.then_inc(vh_turned, 1)

            def scores(h_, par):
                pe.wait_ge(roped, GROUPS * (h_ + 1))
                for g in range(GROUPS):
                    q, k = QK[par][:, g, 0, :], QK[par][:, g, 1, :]
                    nc.tensor.matmul(sc_flat[:, P * g:P * (g + 1)], q[:, 0:P], k[:, 0:P], start=True, stop=True)
                    op = nc.tensor.matmul(sc_flat[:, Q1 + S * g:Q1 + S * (g + 1)], q[:, P:S], k, start=True, stop=True)
                op.then_inc(scored, 1)

            def p_turn(h_):
                pe.wait_ge(normed, 2 * h_ + 2)
                for a, b, c in score_parts:
                    for n in range((b - a) // P):
                        op = nc.tensor.transpose(sc_flat[:, c + P * n:c + P * (n + 1)], sm[:, a + P * n:a + P * (n + 1)],
                                                 ident[:, :])
                op.then_inc(p_turned, 1)

            def attend(h_, par):
                pe.wait_ge(pt_ready, 2 * h_ + 2)
                pe.wait_ge(vh_ready, 2 * (h_ + 1))
                for g in range(GROUPS):
                    nc.tensor.matmul(out_ps[:, 0:P], VT[par][:, g, 0, :], pt[:, P * g:P * (g + 1)],
                                     start=(g == 0), stop=(g == GROUPS - 1))
                for g in range(GROUPS):
                    for n in range(2):
                        c = Q0 + S * g + P * n
                        op = nc.tensor.matmul(out_ps[:, P:S], VT[par][:, g, n, :], pt[:, c:c + P],
                                              start=(g == 0 and n == 0), stop=(g == GROUPS - 1 and n == 1))
                op.then_inc(attended, 1)

            def head(h_, par, before, u, needs=None, first=False):
                for t in range(HEAD_UNITS):
                    m, b = t // 4, t % 4 // 2
                    if t % 4 == 0:
                        pe.wait_ge(pair_summed, P_QKV + HEAD_PAIRS * h_ + m - 1)
                    kts = [(t % 2) * UT + n for n in range(UT)]
                    slot = (t + (0 if par == 0 else HEAD_UNITS)) % RING
                    multiply(u + t, slot, [(acc[(par + m) % 2][:, b, :], X, kt, kt == 0, kt == KT - 1) for kt in kts],
                             needs if t < 2 else None)
                    if first and t == 3:
                        mean_square(2)
                    if before:
                        if t == 0:
                            p_turn(h_ - 1)
                        if t == 1:
                            v_turn(h_ - 1, 1)
                        if t == 3:
                            attend(h_ - 1, 1 - par)
                    if t == 14:
                        scores(h_, par)
                    if t == HEAD_UNITS - 1:
                        v_turn(h_, 0)

            head(0, 0, False, U_QKV, normed_ready(2), first=True)
            with pe.Fori(0, 3) as i:
                for k in range(2):
                    head(2 * i + 1 + k, 1 - k, True, U_QKV + HEAD_UNITS * (1 + k) + 2 * HEAD_UNITS * i)
            last = HEADS - 1
            head(last, 1, True, U_QKV + HEAD_UNITS * last)

            def out_tiles(n, kts):
                return [(acc[n // 2][:, n % 2, :], OX, kt, kt == 0, kt == HEADS - 1) for kt in kts]

            def out_part(n, kts):
                for t, (bank, moving, kt, first, last_tile) in zip(kts, out_tiles(n, kts)):
                    hi, lo = w_hi[n][:, t * P:(t + 1) * P], w_lo[n][:, t * P:(t + 1) * P]
                    if not last_tile:
                        nc.tensor.matmul(bank, hi, moving[:, kt, :], start=first, stop=False)
                        op = nc.tensor.matmul(bank[:, S:2 * S], lo, moving[:, kt, 0:S], start=False, stop=False)
                    else:
                        nc.tensor.matmul(bank[:, S:2 * S], lo, moving[:, kt, 0:S], start=False, stop=False)
                        op = nc.tensor.matmul(bank, hi, moving[:, kt, :], start=False, stop=True)
                return op

            early = range(HEADS - 1)
            pe.wait_ge(lo_ready, U_WO + 1)
            pe.wait_ge(pair_summed, P_WO - 1)
            out_part(0, early)
            p_turn(last)
            pe.wait_ge(lo_ready, U_WO + 2)
            out_part(1, early)
            v_turn(last, 1)
            pe.wait_ge(lo_ready, U_WO + 3)
            pe.wait_ge(pair_summed, P_WO)
            out_part(2, early)
            attend(last, 1)
            pe.wait_ge(o_ready, HEADS)
            for n in range(3):
                out_part(n, [HEADS - 1]).then_inc(units_done, 1)
            multiply(U_WO + 3, 3, out_tiles(3, range(HEADS)))
            with pe.Fori(1, KT // 4) as i:
                two_pairs(U_WO + 4 * i, P_WO + 2 * i, OX, HEADS)
            product(U_F1, P_F1, FB, X, KT, normed_ready(3), 3)
            down(1, U_D1, P_D1)
            def turn(kt, t):
                return nc.tensor.transpose(turned[kt // 4][t][:, P * (kt % 4):P * (kt % 4 + 1)],
                                           Y[:, kt, P * t:P * (t + 1)], ident[:, :])

            pe.wait_ge(y_ready, KT - 1)
            def turn_four(c):
                for t in range(2):
                    for b in range(4):
                        op = turn(4 * c + b, t)
                    op.then_inc(y_turned, 1)

            turn_four(0)
            turn_four(1)
            pe.wait_ge(ss_added, NORM_PAIRS * 5)
            pe.wait_ge(squared, NORM_PAIRS * 4 + POOL_PAIRS + 1)
            for t in range(2):
                parts = [ssum[:, P * t:P * (t + 1)], ssum[:, S + P * t:S + P * (t + 1)], sq[:, 1, P * t:P * (t + 1)]]
                for n, part in enumerate(parts):
                    op = nc.tensor.matmul(fin_ms[:, t:t + 1], part, mean_w[:, 0:1], start=(n == 0), stop=(n == 2))
            op.then_inc(ms_ready, 1)
            turn_four(2)
            pe.wait_ge(y_ready, KT)
            for b in range(4):
                op = turn(12 + b, 0)
            op.then_inc(y_turned, 1)
            pe.wait_ge(fin_rms, 1)
            for b in range(4):
                op = turn(12 + b, 1)
            op.then_inc(y_turned, 1)


def blocks(w):
    k, n = w.shape
    return w.reshape(k // P, P, n // P, P).transpose(2, 0, 1, 3)


def head_order():
    first, second, rest = list(range(HALF)), list(range(HALF, ROT)), list(range(ROT, E))
    return first + rest[:HALF] + second + rest[HALF:]


def stream(a_w_in, a_w_out, b_w_qkv, b_w_o, gate, up, down):
    w_in = blocks(a_w_in)
    ffn = [np.stack([blocks(g), blocks(u)], 1) for g, u in zip(gate, up)]
    qkv = b_w_qkv.reshape(D, 3, GROUPS, HEADS, E).transpose(3, 2, 1, 0, 4)
    qk = qkv[:, :, 0:2][..., np.array(head_order())].reshape(HEADS, 2 * GROUPS, D, E)
    qkv = np.concatenate([qk, qkv[:, :, 2]], 1)
    parts = [w_in[KT:], w_in[:KT], blocks(a_w_out), ffn[0], blocks(down[0]),
             qkv.reshape(-1, P, E), blocks(b_w_o), ffn[1], blocks(down[1])]
    tiles = np.concatenate([p.reshape(-1, P, P) for p in parts])
    return np.ascontiguousarray(tiles.reshape(UNITS, UT, P, P).transpose(0, 2, 1, 3)).reshape(UNITS, P, UC)


def columns(v):
    return v.reshape(-1, P).T


def rope_table():
    inv = np.float32(THETA) ** (-np.arange(0, ROT, 2, dtype=np.float32) / np.float32(ROT))
    ang = (np.arange(S, dtype=np.float32)[:, None] * inv[None, :].astype(np.float32)).T
    table = np.zeros((P, 2, S), np.float32)
    table[:, 0] = 1.0
    table[0:HALF, 0] = table[2 * HALF:3 * HALF, 0] = np.cos(ang)
    table[0:HALF, 1] = -np.sin(ang)
    table[2 * HALF:3 * HALF, 1] = np.sin(ang)
    return table


def mask_table():
    out = []
    for qt in range(2):
        for window, dilation in DILATIONS:
            dist = (P * qt + np.arange(P))[:, None] - np.arange(P * (qt + 1))[None, :]
            seen = (dist >= 0) & (dist <= window) & (dist % dilation == 0)
            out.append(np.where(seen, np.float32(0), np.float32(MASKED)))
    return np.concatenate(out, 1).astype(np.float32)


def kernel(x, a_ln, a_w_in, a_sgu_ln_g, a_sgu_ln_b, a_w_s, a_b_s, a_w_out, b_ln, b_w_qkv, b_w_o,
           ffn_ln, ffn_w_gate, ffn_w_up, ffn_conv_w, ffn_conv_b, ffn_w_down, final_ln):
    import concourse.bacc as bacc
    from concourse.bass_utils import run_bass_kernel_spmd

    f = np.asarray
    conv = [columns(v) for layer in range(2) for v in (*f(ffn_conv_w)[layer], f(ffn_conv_b)[layer])]
    arrays = {
        "w_stream": stream(f(a_w_in)[0], f(a_w_out)[0], f(b_w_qkv)[0], f(b_w_o)[0],
                           f(ffn_w_gate), f(ffn_w_up), f(ffn_w_down)),
        "x_t": f(x)[0].T.reshape(KT, P, S).transpose(1, 0, 2),
        "vecs_d": np.concatenate([columns(f(v)) for v in (a_ln[0], a_sgu_ln_g[0], a_sgu_ln_b[0], b_ln[0], ffn_ln[0],
                                                          ffn_ln[1], final_ln)] + conv, 1),
        "ws_t": f(a_w_s)[0].transpose(2, 0, 1),
        "bs_row": f(a_b_s)[0].reshape(1, -1),
        "mask_d": mask_table(),
        "rope_d": rope_table(),
    }
    nc = bacc.Bacc("TRN2", target_bir_lowering=False, num_devices=1)
    arrays = {name: np.ascontiguousarray(a) for name, a in arrays.items()}
    args = [nc.dram_tensor(name, a.shape, F32, kind="ExternalInput").ap() for name, a in arrays.items()]
    out = nc.dram_tensor("out", (S, D), F32, kind="ExternalOutput").ap()
    trunk(nc, *args, out)
    r = run_bass_kernel_spmd(nc, [arrays], core_ids=[0])
    return np.asarray(r.results[0]["out"]).reshape(1, S, D)
```
